# Optimizing a Trainium2 kernel written in Bass

```python
import math
import jax, jax.numpy as jnp
from jax import lax
import numpy as np

D_MODEL = 1024
BATCH = 1
SEQ = 256
DEPTH = 2

GRID_W = 64
CTX_LEN = 256
N_HEADS = 8
N_KV_HEADS = 2
HEAD_DIM = 64
GROUP = N_HEADS // N_KV_HEADS
ATTN_W = N_HEADS * HEAD_DIM
KV_W = N_KV_HEADS * HEAD_DIM
CONV_W = D_MODEL // 2
CONV_K = 3
WINDOW = 128
BLOCK = 128
D_FF = 2816
ROPE_THETA = 10000.0
EPS = 1e-6
N_MOD = 9
NEG_INF = -1e30
PROJ_SIZES = (ATTN_W, KV_W, KV_W, CONV_W, CONV_W, CONV_W, D_MODEL, D_MODEL)
PROJ_W = ATTN_W + 2 * KV_W + 3 * CONV_W + 2 * D_MODEL

kernel_name = 'hybrid_dit_gqa_sink_shortconv_macaron'

def _split_points(sizes):
    return [int(s) for s in np.cumsum(sizes)[:-1]]

def rmsnorm(x, w):
    xf = x.astype(jnp.float32)
    y = xf * lax.rsqrt(jnp.mean(xf * xf, axis=-1, keepdims=True) + EPS)
    return (y * w.astype(jnp.float32)).astype(x.dtype)

def modulate(h, shift, scale):
    return h * (1 + scale) + shift

def swiglu(h, wi, wo):
    a, g = jnp.split(h @ wi, 2, axis=-1)
    return (jax.nn.silu(g) * a) @ wo

def axial_rope_tables(n_rows):
    row = jnp.broadcast_to(jnp.arange(n_rows)[:, None], (n_rows, GRID_W)).reshape(-1)
    col = jnp.broadcast_to(jnp.arange(GRID_W)[None, :], (n_rows, GRID_W)).reshape(-1)
    n_freq = HEAD_DIM // 4
    inv = ROPE_THETA ** (-jnp.arange(n_freq, dtype=jnp.float32) / n_freq)
    ang_r = row.astype(jnp.float32)[:, None] * inv
    ang_c = col.astype(jnp.float32)[:, None] * inv
    return (jnp.cos(ang_r)[:, None, :], jnp.sin(ang_r)[:, None, :],
            jnp.cos(ang_c)[:, None, :], jnp.sin(ang_c)[:, None, :])

def _rot_half(y, cos, sin):
    y1, y2 = jnp.split(y, 2, axis=-1)
    return jnp.concatenate([y1 * cos - y2 * sin, y2 * cos + y1 * sin], axis=-1)

def apply_axial_rope(t, tables):
    cos_r, sin_r, cos_c, sin_c = tables
    tr, tc = jnp.split(t.astype(jnp.float32), 2, axis=-1)
    out = jnp.concatenate([_rot_half(tr, cos_r, sin_r), _rot_half(tc, cos_c, sin_c)], axis=-1)
    return out.astype(t.dtype)

def _sink_logits(sink, lead_shape, n_q):
    s = sink.astype(jnp.float32).reshape(N_KV_HEADS, GROUP)[:, :, None, None]
    return jnp.broadcast_to(s, tuple(lead_shape) + (N_KV_HEADS, GROUP, n_q, 1))

def windowed_attention_with_context(q, k, v, kc, vc, sink):
    B, S = q.shape[0], q.shape[1]
    nb = S // BLOCK
    L = kc.shape[1]
    scale = HEAD_DIM ** -0.5
    qb = q.reshape(B, nb, BLOCK, N_KV_HEADS, GROUP, HEAD_DIM)
    pad = ((0, 0), (BLOCK, BLOCK), (0, 0), (0, 0))
    kp = jnp.pad(k, pad).reshape(B, nb + 2, BLOCK, N_KV_HEADS, HEAD_DIM)
    vp = jnp.pad(v, pad).reshape(B, nb + 2, BLOCK, N_KV_HEADS, HEAD_DIM)
    kw = jnp.concatenate([kp[:, :-2], kp[:, 1:-1], kp[:, 2:]], axis=2)
    vw = jnp.concatenate([vp[:, :-2], vp[:, 1:-1], vp[:, 2:]], axis=2)
    s_loc = jnp.einsum('bnqkgd,bnjkd->bnkgqj', qb, kw, preferred_element_type=jnp.float32) * scale
    s_ctx = jnp.einsum('bnqkgd,bjkd->bnkgqj', qb, kc, preferred_element_type=jnp.float32) * scale
    blk = jnp.arange(nb)[:, None, None]
    qpos = blk * BLOCK + jnp.arange(BLOCK)[None, :, None]
    kpos = (blk - 1) * BLOCK + jnp.arange(3 * BLOCK)[None, None, :]
    valid = (jnp.abs(kpos - qpos) <= WINDOW) & (kpos >= 0) & (kpos < S)
    s_loc = jnp.where(valid[None, :, None, None], s_loc, NEG_INF)
    logits = jnp.concatenate([s_ctx, s_loc, _sink_logits(sink, (B, nb), BLOCK)], axis=-1)
    p = jax.nn.softmax(logits, axis=-1).astype(v.dtype)
    p_ctx, p_loc = p[..., :L], p[..., L:L + 3 * BLOCK]
    o = (jnp.einsum('bnkgqj,bjkd->bnqkgd', p_ctx, vc)
         + jnp.einsum('bnkgqj,bnjkd->bnqkgd', p_loc, vw))
    return o.reshape(B, S, ATTN_W)

def context_attention(qc, kc, vc, sink):
    B, L = qc.shape[0], qc.shape[1]
    qg = qc.reshape(B, L, N_KV_HEADS, GROUP, HEAD_DIM)
    s = jnp.einsum('bqkgd,bjkd->bkgqj', qg, kc, preferred_element_type=jnp.float32) * (HEAD_DIM ** -0.5)
    logits = jnp.concatenate([s, _sink_logits(sink, (B,), L)], axis=-1)
    p = jax.nn.softmax(logits, axis=-1)[..., :L].astype(vc.dtype)
    return jnp.einsum('bkgqj,bjkd->bqkgd', p, vc).reshape(B, L, ATTN_W)

def short_conv(u, w):
    up = jnp.pad(u, ((0, 0), (1, 1), (0, 0)))
    return up[:, :-2] * w[0] + up[:, 1:-1] * w[1] + up[:, 2:] * w[2]

def gated_merge(o_attn, y_conv, ga, gb, w_oa, w_ob, w_out):
    m = jax.nn.sigmoid(ga) * (o_attn @ w_oa) + jax.nn.sigmoid(gb) * (y_conv @ w_ob)
    return m @ w_out

def trunk_layer(x, xc, c_act, cc_act, tables, w_ada, b_ada, norm_w, ffn1_wi, ffn1_wo, w_in,
                conv_w, sink, w_oa, w_ob, w_out, ffn2_wi, ffn2_wo, last):
    B, S = x.shape[0], x.shape[1]
    L = xc.shape[1]
    mod = (c_act @ w_ada + b_ada).reshape(B, N_MOD, 1, D_MODEL)
    modc = (cc_act @ w_ada + b_ada).reshape(N_MOD, D_MODEL)
    x = x + 0.5 * mod[:, 2] * swiglu(modulate(rmsnorm(x, norm_w[0]), mod[:, 0], mod[:, 1]), ffn1_wi, ffn1_wo)
    xc = xc + 0.5 * modc[2] * swiglu(modulate(rmsnorm(xc, norm_w[0]), modc[0], modc[1]), ffn1_wi, ffn1_wo)
    splits = _split_points(PROJ_SIZES)
    h = modulate(rmsnorm(x, norm_w[1]), mod[:, 3], mod[:, 4])
    hc = modulate(rmsnorm(xc, norm_w[1]), modc[3], modc[4])
    zq, zk, zv, zb, zc, zu, zga, zgb = jnp.split(h @ w_in, splits, axis=-1)
    if last:
        ck, cv = jnp.split(hc @ w_in[:, ATTN_W:ATTN_W + 2 * KV_W], 2, axis=-1)
    else:
        cq, ck, cv, cb, cc, cu, cga, cgb = jnp.split(hc @ w_in, splits, axis=-1)
    kc = ck.reshape(B, L, N_KV_HEADS, HEAD_DIM)
    vc = cv.reshape(B, L, N_KV_HEADS, HEAD_DIM)
    q = apply_axial_rope(zq.reshape(B, S, N_HEADS, HEAD_DIM), tables)
    k = apply_axial_rope(zk.reshape(B, S, N_KV_HEADS, HEAD_DIM), tables)
    v = zv.reshape(B, S, N_KV_HEADS, HEAD_DIM)
    o_attn = windowed_attention_with_context(q, k, v, kc, vc, sink)
    y_conv = zb * short_conv(zc * zu, conv_w)
    x = x + mod[:, 5] * gated_merge(o_attn, y_conv, zga, zgb, w_oa, w_ob, w_out)
    x = x + 0.5 * mod[:, 8] * swiglu(modulate(rmsnorm(x, norm_w[2]), mod[:, 6], mod[:, 7]), ffn2_wi, ffn2_wo)
    if not last:
        oc_attn = context_attention(cq.reshape(B, L, N_HEADS, HEAD_DIM), kc, vc, sink)
        yc_conv = cb * short_conv(cc * cu, conv_w)
        xc = xc + modc[5] * gated_merge(oc_attn, yc_conv, cga, cgb, w_oa, w_ob, w_out)
        xc = xc + 0.5 * modc[8] * swiglu(modulate(rmsnorm(xc, norm_w[2]), modc[6], modc[7]), ffn2_wi, ffn2_wo)
    return x, xc

def setup_inputs(seed: int = 0) -> dict:
    key = jax.random.key(seed)
    ks = jax.random.split(key, 20)

    def nrm(k, shape, scale):
        return jax.random.normal(k, shape, jnp.float32) * scale

    return {
        'x': nrm(ks[0], (BATCH, SEQ, D_MODEL), 1.0),
        'c': nrm(ks[1], (BATCH, D_MODEL), 1.0),
        'ctx': nrm(ks[2], (BATCH, CTX_LEN, D_MODEL), 1.0),
        'c_ctx': nrm(ks[3], (D_MODEL,), 1.0),
        'w_ada': nrm(ks[4], (DEPTH, D_MODEL, N_MOD * D_MODEL), 0.5 * D_MODEL ** -0.5),
        'b_ada': nrm(ks[5], (DEPTH, N_MOD * D_MODEL), 0.02),
        'norm_w': 1.0 + nrm(ks[6], (DEPTH, 3, D_MODEL), 0.02),
        'ffn1_wi': nrm(ks[7], (DEPTH, D_MODEL, 2 * D_FF), D_MODEL ** -0.5),
        'ffn1_wo': nrm(ks[8], (DEPTH, D_FF, D_MODEL), D_FF ** -0.5),
        'w_in': nrm(ks[9], (DEPTH, D_MODEL, PROJ_W), D_MODEL ** -0.5),
        'conv_w': nrm(ks[10], (DEPTH, CONV_K, CONV_W), CONV_K ** -0.5),
        'sink': nrm(ks[11], (DEPTH, N_HEADS), 0.5),
        'w_oa': nrm(ks[12], (DEPTH, ATTN_W, D_MODEL), ATTN_W ** -0.5),
        'w_ob': nrm(ks[13], (DEPTH, CONV_W, D_MODEL), CONV_W ** -0.5),
        'w_out': nrm(ks[14], (DEPTH, D_MODEL, D_MODEL), D_MODEL ** -0.5),
        'ffn2_wi': nrm(ks[15], (DEPTH, D_MODEL, 2 * D_FF), D_MODEL ** -0.5),
        'ffn2_wo': nrm(ks[16], (DEPTH, D_FF, D_MODEL), D_FF ** -0.5),
        'final_norm_w': 1.0 + nrm(ks[17], (D_MODEL,), 0.02),
    }

def reference(x, c, ctx, c_ctx, w_ada, b_ada, norm_w, ffn1_wi, ffn1_wo, w_in, conv_w, sink,
              w_oa, w_ob, w_out, ffn2_wi, ffn2_wo, final_norm_w):
    ROWS = x.shape[1] // GRID_W
    tables = axial_rope_tables(ROWS)
    c_act = jax.nn.silu(c)
    cc_act = jax.nn.silu(c_ctx)
    xc = ctx
    for i in range(DEPTH):
        x, xc = trunk_layer(x, xc, c_act, cc_act, tables, w_ada[i], b_ada[i], norm_w[i],
                            ffn1_wi[i], ffn1_wo[i], w_in[i], conv_w[i], sink[i],
                            w_oa[i], w_ob[i], w_out[i], ffn2_wi[i], ffn2_wo[i],
                            i == DEPTH - 1)
    return rmsnorm(x, final_norm_w)


_drawn_inputs = setup_inputs


def setup_inputs(seed=0):
    import zlib

    import numpy as np

    out = dict(_drawn_inputs(seed))
    spreads = {}
    factors = {'ctx': 3.357, 'norm_w': 4.582, 'sink': 8.0, 'final_norm_w': 2.88}
    for name, (base, spread) in spreads.items():
        noise = np.random.default_rng([zlib.crc32(name.encode()), seed]).standard_normal(out[name].shape)
        drawn = base * np.exp(spread * noise) if base else spread * noise
        out[name] = __import__('jax').numpy.asarray(drawn.astype(out[name].dtype))
    for name, factor in factors.items():
        out[name] = (out[name] * factor).astype(out[name].dtype)
    return out
```

```python
from contextlib import ExitStack

import numpy as np

import concourse.bass as bass
from concourse import mybir

P = 128
F32 = mybir.dt.float32
F32R = mybir.dt.float32r
ALU = mybir.AluOpType
ACT = mybir.ActivationFunctionType
AX_X = mybir.AxisListType.X

D = 1024
DC = D // P
SEQ = 256
CTX = 256
TOK = SEQ + CTX
DEPTH = 2
NMOD = 9
HEADS, KV_HEADS, HD = 8, 2, 64
ATTN_W, KV_W, CONV_W = HEADS * HD, KV_HEADS * HD, D // 2
CC = CONV_W // P
CONV_K = 3
WINDOW = 128
GRID_W = 64
DFF = 2816
FC = DFF // P
GROUPS = FC // 2
EPS = 1e-6
SCALE = HD ** -0.5
NEG = -1e30

Q0 = 0
K0 = ATTN_W
B0 = ATTN_W + 2 * KV_W
C0 = B0 + CONV_W
U0 = C0 + CONV_W
GA0 = U0 + CONV_W
GB0 = GA0 + D

RING = 4
PIECE = 8 * P

V_NORM, V_CONV, V_FIN, V_C = 0, 48, 72, 80
V_BADA = 96
NVEC = V_BADA + DEPTH * NMOD * DC


def shape_constants():
    d = np.arange(P) % HD
    t = np.arange(SEQ)
    pos = np.where((d < HD // 2)[:, None], (t // GRID_W)[None, :], (t % GRID_W)[None, :]).astype(np.float32)
    inv = (np.float32(10000.0) ** (-(d % (HD // 4)).astype(np.float32) / np.float32(HD // 4))).astype(np.float32)
    ang = (pos * inv[:, None]).astype(np.float32)
    rot = np.zeros((P, P))
    for i in range(P):
        if i % (HD // 2) < HD // 4:
            rot[i + HD // 4, i] = -1.0
        else:
            rot[i - HD // 4, i] = 1.0
    q, k = np.arange(P)[:, None], np.arange(P)[None, :]
    pick = np.zeros((P, 2, 2))
    for g in range(4):
        for v in range(2):
            pick[32 * g + v, g % 2, v] = 1.0
    return np.concatenate([np.cos(ang), np.sin(ang), rot, np.eye(P), np.full((P, P), 1.0 / D),
                           np.where(k <= q, 0.0, NEG), np.where(k >= q, 0.0, NEG), pick.reshape(P, 4)], axis=1).astype(np.float32)


N_CONST = 2 * SEQ + 5 * P + 4

WI_P, WO_P, OA_P, OB_P, OUT_P = 4 * GROUPS, FC, CC, CC, DC
UNITS = ["q0", "q1", "kv", "c0", "u0", "b0", "c1", "u1", "b1"] + [f"g{i}" for i in range(8)]
PROJ_P = 2 * len(UNITS)
ACT_UNITS = [u for u, k in enumerate(UNITS) if k[0] in "qkcg"]
DVE_UNITS = [u for u, k in enumerate(UNITS) if k[0] in "ub"]


def piece_plan():
    first, n, ways = {}, 0, []
    for l in range(DEPTH):
        for name, count in (("wi1", WI_P), ("wo1", WO_P), ("proj", PROJ_P), ("oa", OA_P), ("ob", OB_P),
                            ("out", OUT_P), ("wi2", WI_P), ("wo2", WO_P)):
            first[name, l] = n
            ways += [4 if name == "proj" and j < 4 else 2 if name == "oa" else 1 for j in range(count)]
            n += count
    at, loaded = [0] * RING, []
    for j, w in enumerate(ways):
        at[j % RING] += 16 * w
        loaded.append(at[j % RING])
    return first, loaded, n


FIRST, LOADED, PIECES = piece_plan()
ADA_IN_FFN = {0: (2, 7), 1: (9, 9)}
STEP_HEAD = [b + 4 * r for b in range(4) for r in range(2)]


def bank_of(m):
    return (m + 4) % 8


def build(nc, x, c, ctx, c_ctx, w_ada, b_ada, norm_w, ffn1_wi, ffn1_wo, w_in, conv_w, sink, w_oa, w_ob, w_out,
          ffn2_wi, ffn2_wo, final_norm_w, consts, out):
    stack = ExitStack()
    with stack:
        def sb(name, shape, dt=F32):
            return stack.enter_context(nc.sbuf_tensor(name, shape, dt))

        def sem(name):
            return stack.enter_context(nc.semaphore(name))

        X = sb("X", [P, DC, TOK])
        hH = sb("hH", [P, DC, TOK], F32R)
        hL = sb("hL", [P, DC, TOK], F32R)
        raw = sb("raw", [P, RING, PIECE])
        wH = sb("wH", [P, RING, PIECE], F32R)
        wL = sb("wL", [P, RING, PIECE], F32R)
        T = sb("T", [P, 4, TOK])
        cst = sb("cst", [P, N_CONST])
        VT = sb("VT", [P, NVEC])
        mod = sb("mod", [P, DEPTH * NMOD, DC, 2])
        normA = sb("normA", [P, 3 * DEPTH, DC, 2])
        gateH = sb("gateH", [P, 3 * DEPTH, DC, 2])
        cact = sb("cact", [P, 2, DC])
        sinkP = sb("sinkP", [P, DEPTH * HEADS])
        sinkN = sb("sinkN", [P, DEPTH * HEADS])
        epsT = sb("epsT", [P, 1])
        stat = sb("stat", [P, 6, 4])
        with ExitStack() as r:
            adaA = r.enter_context(nc.sbuf_tensor("adaA", [P, 2, D], F32))
            with ExitStack() as s:
                GH = s.enter_context(nc.sbuf_tensor("GH", [P, FC, TOK], F32R))
                GL = s.enter_context(nc.sbuf_tensor("GL", [P, FC, TOK], F32R))
            with ExitStack() as s:
                s.enter_context(nc.sbuf_tensor("hidden_front", [P, FC - 4, TOK], F32))
                rowS = s.enter_context(nc.sbuf_tensor("rowS", [P, TOK], F32))
                s.enter_context(nc.sbuf_tensor("hidden_mid", [P, 3 + FC - 4, TOK], F32))
                adaB = s.enter_context(nc.sbuf_tensor("adaB", [P, 2, D], F32))
            with ExitStack() as s:
                def mb(name, shape, dt=F32):
                    return s.enter_context(nc.sbuf_tensor(name, shape, dt))
                QH = mb("QH", [P, 4, TOK], F32R)
                QL = mb("QL", [P, 4, TOK], F32R)
                KH = mb("KH", [P, TOK], F32R)
                KL = mb("KL", [P, TOK], F32R)
                V32 = mb("V32", [P, TOK])
                VH = mb("VH", [P, 4, P], F32R)
                VL = mb("VL", [P, 4, P], F32R)
                YH = mb("YH", [P, CC, TOK], F32R)
                YL = mb("YL", [P, CC, TOK], F32R)
                GA = mb("GA", [P, DC, TOK])
                PTH = mb("PTH", [P, 3, TOK], F32R)
                PTL = mb("PTL", [P, 3, TOK], F32R)
                with ExitStack() as s2:
                    GB = s2.enter_context(nc.sbuf_tensor("GB", [P, DC, TOK], F32))
                cC = mb("cC", [P, 2, TOK])
                cU = mb("cU", [P, 2, 2, SEQ + 2])
                cY = mb("cY", [P, 2, TOK])
                ropeT = mb("ropeT", [P, 2, SEQ])
            with ExitStack() as s:
                xin = s.enter_context(nc.sbuf_tensor("xin", [P, 4, D], F32))
                vin = s.enter_context(nc.sbuf_tensor("vin", [P, 3, P], F32))
            with ExitStack() as s:
                yout = s.enter_context(nc.sbuf_tensor("yout", [P, 2, D], F32))
        ps = [stack.enter_context(nc.psum_tensor(f"ps{i}", [P, TOK], F32)) for i in range(8)]

        cosT, sinT = cst[:, 0:SEQ], cst[:, SEQ:2 * SEQ]
        o = 2 * SEQ
        pick = cst[:, N_CONST - 4:].rearrange("p (h v) -> p h v", h=2)
        ada = [adaA[:, 0], adaA[:, 1], adaB[:, 0], adaB[:, 1]]
        rotM, ident, meanM, mask0, mask1 = (cst[:, o + j * P:o + (j + 1) * P] for j in range(5))

        loaded = [sem(f"loaded{i}") for i in range(RING)]
        hi_done = sem("hi_done")
        lo_done = sem("lo_done")
        w_used = sem("w_used")
        in_vec, in_x, in_c, in_sink = sem("in_vec"), sem("in_x"), sem("in_c"), sem("in_sink")
        ada_loaded = [sem(f"ada_loaded{i}") for i in range(4)]
        ada_used = sem("ada_used")
        bank5_zero = sem("bank5_zero")
        row_out = sem("row_out")
        ada_T = sem("ada_T")
        ada_out = sem("ada_out")
        vec_T, vec_out, c_silu = sem("vec_T"), sem("vec_out"), sem("c_silu")
        x_T = sem("x_T")
        x_ready = sem("x_ready")
        sq_done, sq_used = sem("sq_done"), sem("sq_used")
        rms = sem("rms")
        hp_done = sem("hp_done")
        h_hi, h_lo = sem("h_hi"), sem("h_lo")
        a_out, g_silu = sem("a_out"), sem("g_silu")
        g_prod, g_hi, g_lo = sem("g_prod"), sem("g_hi"), sem("g_lo")
        acc_mm = sem("acc_mm")
        oa_out, ob_out, ob_sum = sem("oa_out"), sem("ob_out"), sem("ob_sum")
        m_hi, m_lo = sem("m_hi"), sem("m_lo")
        proj_act, proj_dve = sem("proj_act"), sem("proj_dve")
        rope_mm, rope_done, q_hi, q_lo = sem("rope_mm"), sem("rope_done"), sem("q_hi"), sem("q_lo")
        v_T, v_hi, v_lo = sem("v_T"), sem("v_hi"), sem("v_lo")
        y_hi, y_lo = sem("y_hi"), sem("y_lo")
        s_mm, s_max, p_exp, p_norm = sem("s_mm"), sem("s_max"), sem("p_exp"), sem("p_norm")
        pt_mm, pt_hi, pt_lo = sem("pt_mm"), sem("pt_hi"), sem("pt_lo")
        pv_mm, o_hi, o_lo = sem("pv_mm"), sem("o_hi"), sem("o_lo")
        vec_step = sem("vec_step")
        fin_ready, fin_T, fin_out, stored = sem("fin_ready"), sem("fin_T"), sem("fin_out"), sem("stored")

        def wait(eng, s, v):
            if not isinstance(v, int) or v > 0:
                eng.wait_ge(s, v)

        T_AFTER = [TOK, TOK, TOK, TOK, TOK, SEQ, SEQ]
        T_NORM = [TOK, TOK, TOK, TOK, TOK, SEQ, SEQ]

        def halves(t):
            return t // SEQ

        def x_count(r, m):
            n = sum(DC * (1 if q == 0 else halves(T_AFTER[q])) for q in range(r))
            return n + (m + 1) * (1 if r == 0 else halves(T_AFTER[r]))

        def h_count(v, m):
            return sum(DC * halves(T_NORM[q]) for q in range(v)) + (m + 1) * halves(T_NORM[v])

        def tiles(l):
            return 3 if l == 0 else 2

        def tile_count(l, s, j):
            return (0 if l == 0 else 8 * 3) + s * tiles(l) + j + 1

        def wait_chunk(eng, l, name, m):
            idx = ("wo1", "oa", "ob", "out", "wo2").index(name)
            if m < DC - 1:
                eng.wait_ge(acc_mm, (DC - 1) * (5 * l + idx) + m + 1)
            else:
                pieces = {"wo1": WO_P, "oa": OA_P, "ob": OB_P, "out": OUT_P, "wo2": WO_P}[name]
                eng.wait_ge(w_used, FIRST[name, l] + pieces)

        block = stack.enter_context(nc.Block())

        @block.sync
        def _(sp):
            sp.dma_start(vin[0:48, 0, :], norm_w.rearrange("l j (k p) -> (l j k) p", p=P)).then_inc(in_vec, 16)
            sp.dma_start(vin[V_CONV:72, 0, :], conv_w.rearrange("l j (k p) -> (l j k) p", p=P)).then_inc(in_vec, 16)
            sp.dma_start(vin[V_FIN:80, 0, :], final_norm_w.rearrange("(k p) -> k p", p=P)).then_inc(in_vec, 16)
            sp.dma_start(vin[V_C:88, 0, :], c.rearrange("b (k p) -> (b k) p", p=P)).then_inc(in_vec, 16)
            sp.dma_start(vin[88:96, 0, :], c_ctx.rearrange("(k p) -> k p", p=P)).then_inc(in_vec, 16)
            for l in range(DEPTH):
                sp.dma_start(vin[0:NMOD * DC, 1 + l, :],
                             b_ada[l].rearrange("(k p) -> k p", p=P)).then_inc(in_vec, 16)
            sp.dma_start(cst[:], consts).then_inc(in_c, 16)
            sp.dma_start(xin[:, 0:2, :], x[0].rearrange("(t p) d -> p t d", p=P)).then_inc(in_x, 16)
            sp.dma_start(xin[:, 2:4, :], ctx[0].rearrange("(t p) d -> p t d", p=P)).then_inc(in_x, 16)
            sp.dma_start(sinkP[:], sink.rearrange("l h -> (l h)").partition_broadcast(P)).then_inc(in_sink, 16)

            def slot_free(n0, j, i=0):
                if isinstance(i, int):
                    wait(sp, lo_done, n0 + j + 4 * i - RING + 1)
                else:
                    sp.wait_ge(lo_done, i * 4 + (n0 + j - RING + 1))

            def load_columns(n0, j, src, kh, col, i=0):
                slot_free(n0, j, i)
                s = (n0 + j) % RING
                sp.dma_start(raw[:, s, :].rearrange("p (k n) -> p k n", k=4),
                             src.rearrange("(k p) n -> p k n", p=P)[:, 4 * kh:4 * kh + 4, bass.ds(col, 2 * P)]
                             ).then_inc(loaded[s], 16)

            def load_rows(n0, j, src, k, i=0):
                slot_free(n0, j, i)
                s = (n0 + j) % RING
                sp.dma_start(raw[:, s, :], src[bass.ds(k * P, P), :]).then_inc(loaded[s], 16)

            def ffn_loads(l, name, wi, wo):
                n0 = FIRST["wi" + name, l]

                def group(i):
                    for j in range(4):
                        load_columns(n0, j, wi, j % 2, i * (2 * P) + (j // 2) * DFF, i)
                group(0)
                with sp.Fori(1, GROUPS) as i:
                    group(i)
                n0 = FIRST["wo" + name, l]
                with sp.Fori(0, FC // RING) as i:
                    for j in range(RING):
                        load_rows(n0, j, wo, i * RING + j, i)
                for j in range(FC // RING * RING, FC):
                    load_rows(n0, j, wo, j)

            for l in range(DEPTH):
                ffn_loads(l, "1", ffn1_wi[l], ffn1_wo[l])
                n0 = FIRST["proj", l]
                wv = w_in[l].rearrange("(k p) n -> p k n", p=P)
                for u, kind in enumerate(UNITS[:9]):
                    i = int(kind[1]) if kind != "kv" else 0
                    for kh in range(2):
                        if kind[0] == "q":
                            n = n0 + 2 * u + kh
                            slot_free(n, 0)
                            dst = raw[:, n % RING, :].rearrange("p (k b r d) -> p k b r d", k=4, b=2, r=2)
                            for b in range(2):
                                for r in range(2):
                                    col = Q0 + (2 * i + b + 4 * r) * HD
                                    sp.dma_start(dst[:, :, b, r, :], wv[:, 4 * kh:4 * kh + 4, col:col + HD]
                                                 ).then_inc(loaded[n % RING], 16)
                        else:
                            col = {"k": K0, "b": B0, "c": C0, "u": U0}[kind[0]] + 2 * P * i
                            load_columns(n0 + 2 * u + kh, 0, w_in[l], kh, col)
                with sp.Fori(0, 4) as i:
                    for j in range(4):
                        load_columns(n0 + 18, j, w_in[l], j % 2, i * (4 * P) + (j // 2) * 2 * P + GA0, i)
                for b in range(4):
                    n = FIRST["oa", l] + b
                    slot_free(n, 0)
                    for r in range(2):
                        sp.dma_start(raw[r * HD:(r + 1) * HD, n % RING, :],
                                     w_oa[l, (b + 4 * r) * HD:(b + 4 * r + 1) * HD, :]).then_inc(loaded[n % RING], 16)
                for k in range(4):
                    load_rows(FIRST["ob", l], k, w_ob[l], k)
                for k in range(DC):
                    load_rows(FIRST["out", l], k, w_out[l], k)
                ffn_loads(l, "2", ffn2_wi[l], ffn2_wo[l])
            for tb in range(2):
                sp.wait_ge(fin_out, 2 * tb + 2)
                sp.dma_start(out[0, tb * P:(tb + 1) * P, :], yout[:, tb, :]).then_inc(stored, 16)
            sp.wait_ge(stored, 32)

        @block.gpsimd
        def _(pool):
            def load_ada(mi, k, base, i=None):
                l, j = mi
                need = 4 * base + k // 2 - 1
                if i is None:
                    wait(pool, ada_used, need)
                    src = w_ada[l, k * P:(k + 1) * P, j * D:(j + 1) * D]
                else:
                    pool.wait_ge(ada_used, i * 4 + need)
                    src = w_ada[l, k * P:(k + 1) * P, bass.ds(i * D + j * D, D)]
                pool.dma_start(ada[k % 4], src).then_inc(ada_loaded[k % 4], 16)

            for j in range(2):
                for k in range(DC):
                    load_ada((0, j), k, j)
            with pool.Fori(0, 7) as i:
                for k in range(DC):
                    load_ada((0, 2), k, 2, i)
            pool.wait_ge(m_lo, 8)
            with pool.Fori(0, NMOD) as i:
                for k in range(DC):
                    load_ada((1, 0), k, 9, i)

        @block.tensor
        def _(pe):
            mm = nc.tensor.matmul

            def triple(dst, wa, wb, ra, rb, start, stop, group_check=True):
                kw = {} if group_check else {"skip_group_check": True}
                mm(dst, wa, ra, start=start, stop=False, **kw)
                mm(dst, wa, rb, start=False, stop=False, **kw)
                return mm(dst, wb, ra, start=False, stop=stop, **kw)

            def ada_pair(p, base, i=None):
                for k in (2 * p, 2 * p + 1):
                    count = 16 * (2 * base + k // 4 + 1)
                    pe.wait_ge(ada_loaded[k % 4], count if i is None else i * 32 + count)
                if p == 0:
                    if i is None:
                        wait(pe, row_out, base)
                    else:
                        pe.wait_ge(row_out, i + base)
                for k in (2 * p, 2 * p + 1):
                    for h in range(2):
                        g = 2 * (k % 2) + h
                        last = mm(ps[5][32 * g:32 * g + 2, :], cact[:, :, k], ada[k % 4][:, h * TOK:(h + 1) * TOK],
                                  start=(p == 0), stop=(p == 3), skip_group_check=True)
                last.then_inc(ada_used, 1)

            def ada_turn(base, i=None):
                pe.wait_ge(row_out, base + 1 if i is None else i + (base + 1))
                if i is None:
                    wait(pe, ada_out, base)
                else:
                    pe.wait_ge(ada_out, i + base)
                for m in range(DC):
                    last = mm(ps[6][:, 2 * m:2 * m + 2], rowS[:, (m % 4) * P:(m % 4 + 1) * P], pick[:, m // 4, :],
                              start=True, stop=True)
                last.then_inc(ada_T, 1)

            def columns_piece(n0, j, banks, kh, t, i=0, v=None):
                s = (n0 + j) % RING
                pe.wait_ge(lo_done, i * 4 + (n0 + j + 1))
                for k in range(4):
                    kk = 4 * kh + k
                    if v is not None:
                        pe.wait_ge(h_lo, h_count(v, kk))
                    for b in range(2):
                        w = slice(k * 2 * P + b * P, k * 2 * P + (b + 1) * P)
                        last = triple(ps[banks + b][:, 0:t], wH[:, s, w], wL[:, s, w], hH[:, kk, 0:t], hL[:, kk, 0:t],
                                      kk == 0, kk == DC - 1, False)
                last.then_inc(w_used, 1)

            def rows_piece(n0, j, k, ra, rb, t, start, stop, i=0, bank_wait=None):
                s = (n0 + j) % RING
                pe.wait_ge(lo_done, i * 4 + (n0 + j + 1))
                for m in range(DC):
                    if bank_wait is not None:
                        bank_wait(m)
                    last = triple(ps[bank_of(m)][:, 0:t], wH[:, s, m * P:(m + 1) * P], wL[:, s, m * P:(m + 1) * P],
                                  ra[:, bass.ds(k, 1), 0:t].rearrange("p a t -> p (a t)") if not isinstance(k, int) else ra[:, k, 0:t],
                                  rb[:, bass.ds(k, 1), 0:t].rearrange("p a t -> p (a t)") if not isinstance(k, int) else rb[:, k, 0:t],
                                  start, stop, False)
                    if stop and m < DC - 1:
                        last.then_inc(acc_mm, 1)
                last.then_inc(w_used, 1)

            def sum_squares(v):
                t = T_NORM[v]
                wait(pe, x_ready, x_count(v, 0))
                for m in range(DC):
                    pe.wait_ge(sq_done, DC * v + m + 1)
                    mm(ps[4][:, 0:t], meanM, T[:, m % 2, 0:t], start=(m == 0), stop=(m == DC - 1)).then_inc(sq_used, 1)

            def ffn(f, v):
                l, name = f // 2, "12"[f % 2]
                t = T_NORM[v]
                n0 = FIRST["wi" + name, l]

                def group(i, ada_base=None, turn_base=None):
                    if isinstance(i, int) and i == 0:
                        wait(pe, x_ready, x_count(v, DC - 1))
                    else:
                        pe.wait_ge(a_out, i * 2 + 2 * GROUPS * f)
                    for j in range(4):
                        if j == 2 and not (isinstance(i, int) and i == 0):
                            pe.wait_ge(g_silu, i * 2 + 2 * GROUPS * f)
                        columns_piece(n0, j, 2 * (j // 2), j % 2, t, i,
                                      v if isinstance(i, int) and i == 0 and j < 2 else None)
                        if ada_base is not None:
                            if isinstance(i, int):
                                ada_pair(j, ada_base + i)
                            else:
                                ada_pair(j, ada_base, i)
                        if turn_base is not None and j == 0:
                            if isinstance(i, int):
                                ada_turn(turn_base + i - 1)
                            else:
                                ada_turn(turn_base - 1, i)

                ada0, count = ADA_IN_FFN.get(f, (None, 0))
                if count:
                    pe.wait_ge(bank5_zero, f + 1)
                group(0, ada0)
                if count:
                    with pe.Fori(1, count) as i:
                        group(i, ada0, ada0)
                    group(count, None, ada0)
                if count + 1 < GROUPS:
                    with pe.Fori(max(count, 0) + 1, GROUPS) as i:
                        group(i)
                n0 = FIRST["wo" + name, l]
                if count:
                    pe.wait_ge(ada_out, ada0 + count)

                def bank_wait(m):
                    if m == 4:
                        pe.wait_ge(a_out, 2 * GROUPS * (f + 1))
                    if m == 6:
                        pe.wait_ge(g_silu, 2 * GROUPS * (f + 1))
                pe.wait_ge(g_lo, 2 * GROUPS * (f + 1) - 2)
                for j in range(RING):
                    rows_piece(n0, j, j, GH, GL, t, j == 0, False, bank_wait=bank_wait if j == 0 else None)
                with pe.Fori(1, FC // RING) as i:
                    for j in range(RING):
                        rows_piece(n0, j, i * RING + j, GH, GL, t, False, False, i)
                pe.wait_ge(g_lo, 2 * GROUPS * (f + 1))
                for j in range(FC // RING * RING, FC):
                    rows_piece(n0, j, j, GH, GL, t, False, j == FC - 1)

            def rope(l, bi):
                if bi < 4:
                    pe.wait_ge(proj_act, 26 * l + bi + 1)
                else:
                    pe.wait_ge(proj_act, 26 * l + 5)
                if bi >= 2:
                    pe.wait_ge(rope_done, 5 * l + bi - 1)
                mm(ps[4 + bi % 2][:, 0:SEQ], rotM, T[:, bi % 4, 0:SEQ], start=True, stop=True).then_inc(rope_mm, 1)

            def unit_banks_free(l, u):
                if u >= 2:
                    p = u - 2
                    if p in ACT_UNITS:
                        pe.wait_ge(proj_act, 26 * l + 2 * ACT_UNITS.index(p) + 2)
                    else:
                        pe.wait_ge(proj_dve, 8 * l + 2 * DVE_UNITS.index(p) + 2)

            def scores(l, s):
                b, r = s // 2, s % 2
                rows = slice(r * HD, (r + 1) * HD)
                if s == 0:
                    pe.wait_ge(q_lo, 5 * (l + 1))
                    pe.wait_ge(v_lo, l + 1)
                for j in range(tiles(l)):
                    if s > 0:
                        pe.wait_ge(pt_lo, tile_count(l, s - 1, j))
                    for q in range(2 if j == 2 else 1):
                        tq = j + q
                        qs = slice(tq * P, (tq + 1) * P)
                        keys = slice(0, TOK) if j < 2 else slice(SEQ, TOK)
                        dst = ps[4 + j][:, 0:TOK] if j < 2 else ps[6][:, q * CTX:(q + 1) * CTX]
                        last = triple(dst, QH[rows, b, qs], QL[rows, b, qs], KH[rows, keys], KL[rows, keys], True, True)
                    last.then_inc(s_mm, 1)

            def transpose_probs(l, s):
                for j in range(tiles(l)):
                    pe.wait_ge(p_norm, tile_count(l, s, j))
                    for q in range(4):
                        src = T[:, j, q * P:(q + 1) * P] if j < 2 else \
                            T[:, 2, (q % 2) * CTX + (q // 2) * P:(q % 2) * CTX + (q // 2 + 1) * P]
                        last = nc.tensor.transpose(ps[4 + j][:, q * P:(q + 1) * P], src, ident)
                    last.then_inc(pt_mm, 1)

            def weigh_values(l, s):
                pe.wait_ge(pt_lo, tile_count(l, s, tiles(l) - 1))
                if s > 0:
                    pe.wait_ge(o_lo, 8 * l + s)
                for kb in range(4):
                    ks = slice(kb * P, (kb + 1) * P)
                    last = triple(ps[7][:, 0:SEQ].rearrange("p (t q) -> p t q", t=2), VH[:, kb, :], VL[:, kb, :],
                                  PTH[:, 0:2, ks], PTL[:, 0:2, ks], kb == 0, kb == 3)
                if l == 0:
                    for kb in range(2):
                        ks = slice(kb * CTX, (kb + 1) * CTX)
                        last = triple(ps[7][:, SEQ:TOK], VH[:, 2 + kb, :], VL[:, 2 + kb, :],
                                      PTH[:, 2, ks], PTL[:, 2, ks], kb == 0, kb == 1)
                last.then_inc(pv_mm, 1)

            def mixers(l):
                v = 3 * l + 1
                t = TOK if l == 0 else SEQ
                n0 = FIRST["proj", l]
                pe.wait_ge(x_ready, x_count(v, DC - 1))
                for u in range(9):
                    unit_banks_free(l, u)
                    for kh in range(2):
                        columns_piece(n0 + 2 * u + kh, 0, 2 * (u % 2), kh, TOK if UNITS[u] == "kv" else t,
                                      v=v if u == 0 else None)
                    if u in (1, 2):
                        rope(l, 2 * u - 2)
                        rope(l, 2 * u - 1)
                    if u == 3:
                        rope(l, 4)
                        pe.wait_ge(proj_act, 26 * l + 6)
                        for tb in range(4):
                            last = nc.tensor.transpose(ps[6][:, tb * P:(tb + 1) * P], V32[:, tb * P:(tb + 1) * P], ident)
                        last.then_inc(v_T, 1)
                for s in range(8):
                    u = 9 + s
                    scores(l, s)
                    unit_banks_free(l, u)
                    columns_piece(n0 + 2 * u, 0, 2 * (u % 2), 0, t)
                    transpose_probs(l, s)
                    columns_piece(n0 + 2 * u + 1, 0, 2 * (u % 2), 1, t)
                    weigh_values(l, s)

                def oa_bank(m):
                    if m == 0:
                        pe.wait_ge(o_lo, 8 * (l + 1))
                        pe.wait_ge(proj_act, 26 * (l + 1))
                for k in range(4):
                    rows_piece(FIRST["oa", l] + k, 0, k, QH, QL, t, k == 0, k == 3, bank_wait=oa_bank if k == 0 else None)

                def ob_bank(m):
                    pe.wait_ge(oa_out, 8 * l + m + 1)
                pe.wait_ge(y_lo, 4 * (l + 1))
                for k in range(4):
                    rows_piece(FIRST["ob", l] + k, 0, k, YH, YL, t, k == 0, k == 3, bank_wait=ob_bank if k == 0 else None)

                def out_bank(m):
                    pe.wait_ge(ob_out, 8 * l + m + 1)
                for k in range(DC):
                    pe.wait_ge(m_lo, 8 * l + k + 1)
                    rows_piece(FIRST["out", l] + k, 0, k, hH, hL, t, k == 0, k == DC - 1,
                               bank_wait=out_bank if k == 0 else None)

            pe.wait_ge(in_c, 16)
            pe.wait_ge(in_vec, 16 * 7)
            nc.tensor.transpose(ps[6][:, 0:96], vin[0:96, 0, :], ident[0:96, 0:96])
            for l in range(DEPTH):
                last = nc.tensor.transpose(ps[6][:, 96 + 72 * l:96 + 72 * (l + 1)], vin[0:72, 1 + l, :],
                                           ident[0:72, 0:72])
            last.then_inc(vec_T, 1)
            pe.wait_ge(in_x, 32)
            for m in range(DC):
                if m >= 4:
                    pe.wait_ge(x_ready, m - 3)
                for tb in range(4):
                    last = nc.tensor.transpose(ps[m % 4][:, tb * P:(tb + 1) * P], xin[:, tb, m * P:(m + 1) * P], ident)
                last.then_inc(x_T, 1)
            sum_squares(0)
            pe.wait_ge(c_silu, 1)
            pe.wait_ge(bank5_zero, 1)
            pe.wait_ge(vec_out, 1)
            for j in range(2):
                for p in range(4):
                    ada_pair(p, j)
                ada_turn(j)

            for l in range(DEPTH):
                ffn(2 * l, 3 * l)
                sum_squares(3 * l + 1)
                mixers(l)
                sum_squares(3 * l + 2)
                ffn(2 * l + 1, 3 * l + 2)
                sum_squares(3 * l + 3)
            for m in range(DC):
                pe.wait_ge(fin_ready, m + 1)
                for tb in range(2):
                    nc.tensor.transpose(ps[2 * tb + m // 4][:, (m % 4) * P:(m % 4 + 1) * P],
                                        T[:, m % 2, tb * P:(tb + 1) * P], ident).then_inc(fin_T, 1)

        @block.scalar
        def _(act):
            av = nc.scalar.activation

            def hi(n0, j=0, i=0):
                s = (n0 + j) % RING
                if n0 + j >= PIECES and isinstance(i, int):
                    return
                if isinstance(i, int):
                    act.wait_ge(loaded[s], LOADED[n0 + j + 4 * i])
                    wait(act, w_used, n0 + j + 4 * i - RING + 1)
                else:
                    act.wait_ge(loaded[s], i * 16 + LOADED[n0 + j])
                    act.wait_ge(w_used, i * 4 + (n0 + j - RING + 1))
                av(wH[:, s, :], raw[:, s, :], ACT.Copy).then_inc(hi_done, 1)

            def norm_act(v, n0):
                t = T_NORM[v]
                for m in range(DC):
                    act.wait_ge(x_ready, x_count(v, m))
                    if m >= 2:
                        act.wait_ge(sq_used, DC * v + m - 1)
                    av(T[:, m % 2, 0:t], X[:, m, 0:t], ACT.Square).then_inc(sq_done, 1)
                act.wait_ge(sq_used, DC * (v + 1))
                av(T[:, 2, 0:t], ps[4][:, 0:t], ACT.Sqrt, bias=epsT[:, 0:1]).then_inc(rms, 1)
                if v == 6:
                    return
                shift = 9 * (v // 3) + 3 * (v % 3)
                for m in range(DC):
                    for hf in range(halves(t)):
                        c0 = h_count(v, m) - halves(t) + hf + 1
                        cs = slice(hf * SEQ, (hf + 1) * SEQ)
                        act.wait_ge(hp_done, c0)
                        av(hH[:, m, cs], T[:, m % 2, cs], ACT.Identity, bias=mod[:, shift, m, hf:hf + 1]).then_inc(h_hi, 1)
                    if m == 3:
                        hi(n0 + 2)
                    if m == 6:
                        hi(n0 + 3)

            def silu_evac(f, t, i):
                static = isinstance(i, int)
                for b in range(2):
                    act.wait_ge(w_used, i * RING + (FIRST["wi" + "12"[f % 2], f // 2] + 4))
                    wait(act, g_lo, i * 2 + 2 * GROUPS * f)
                    av(T[:, 2 + b, 0:t], ps[2 + b][:, 0:t], ACT.Silu).then_inc(g_silu, 1)
                for b in range(2):
                    act.wait_ge(g_prod, i * 2 + (2 * GROUPS * f + b + 1))
                    if static:
                        dst = GH[:, 2 * i + b, 0:t]
                    else:
                        dst = GH[:, bass.ds(i * 2 + b, 1), 0:t].rearrange("p a t -> p (a t)")
                    av(dst, T[:, 2 + b, 0:t], ACT.Copy).then_inc(g_hi, 1)

            def ffn_act(f, v):
                l, name = f // 2, "12"[f % 2]
                t = T_NORM[v]
                n0 = FIRST["wi" + name, l]

                n0w = n0

                def value_evac(i):
                    for b in range(2):
                        act.wait_ge(w_used, i * RING + (n0w + 2))
                        av(T[:, b, 0:t], ps[b][:, 0:t], ACT.Copy).then_inc(a_out, 1)

                def group(i):
                    hi(n0, 2, i)
                    hi(n0, 3, i)
                    silu_evac(f, t, i - 1)
                    hi(n0, 4, i)
                    hi(n0, 5, i)
                    value_evac(i)
                hi(n0, 4)
                hi(n0, 5)
                value_evac(0)
                group(1)
                with act.Fori(2, GROUPS - 1) as i:
                    group(i)
                i = GROUPS - 1
                hi(n0 + 4 * i + 2)
                hi(n0 + 4 * i + 3)
                silu_evac(f, t, i - 1)
                hi(n0 + 4 * i + 4)
                hi(n0 + 4 * i + 5)
                value_evac(i)
                silu_evac(f, t, i)
                n0 = FIRST["wo" + name, l]
                with act.Fori(0, FC // RING) as i:
                    for j in range(RING):
                        hi(n0, 2 + j, i)
                for j in range(FC // RING * RING, FC):
                    hi(n0 + 2 + j)

            def mixers_act(l):
                t = TOK if l == 0 else SEQ
                n0 = FIRST["proj", l]
                a0 = 26 * l
                for u in range(9):
                    kind = UNITS[u]
                    if u > 0:
                        hi(n0 + 2 * u + 2)
                        hi(n0 + 2 * u + 3)
                    if u in (1, 2):
                        for bi in (2 * u - 2, 2 * u - 1):
                            act.wait_ge(rope_done, 5 * l + bi + 1)
                            av(QH[:, bi, 0:t], T[:, bi, 0:t], ACT.Copy).then_inc(q_hi, 1)
                    if u == 3:
                        act.wait_ge(rope_done, 5 * l + 5)
                        av(KH[:], T[:, 0, :], ACT.Copy).then_inc(q_hi, 1)
                        act.wait_ge(v_T, l + 1)
                        av(VH[:].rearrange("p b d -> p (b d)"), ps[6][:], ACT.Copy).then_inc(v_hi, 1)
                    if u == 6:
                        for b in range(2):
                            act.wait_ge(proj_dve, 8 * l + 2 * DVE_UNITS.index(5) + b + 1)
                            av(YH[:, b, 0:t], cY[:, b, 0:t], ACT.Copy).then_inc(y_hi, 1)
                    if u in ACT_UNITS:
                        act.wait_ge(w_used, n0 + 2 * u + 2)
                        if kind[0] == "q":
                            for b in range(2):
                                av(T[:, 2 * u + b, 0:t], ps[2 * (u % 2) + b][:, 0:t], ACT.Copy).then_inc(proj_act, 1)
                        elif kind == "kv":
                            act.wait_ge(q_lo, 5 * l + 1)
                            av(T[:, 0, :], ps[0][:], ACT.Copy).then_inc(proj_act, 1)
                            av(V32[:], ps[1][:], ACT.Copy).then_inc(proj_act, 1)
                        else:
                            if u == 6:
                                act.wait_ge(y_lo, 4 * l + 2)
                            for b in range(2):
                                av(cC[:, b, 0:t], ps[2 * (u % 2) + b][:, 0:t], ACT.Copy).then_inc(proj_act, 1)
                for s in range(8):
                    u = 9 + s
                    h = HEADS * l + STEP_HEAD[s]
                    hi(n0 + 2 * u + 2)
                    if s == 0:
                        for b in range(2):
                            act.wait_ge(proj_dve, 8 * l + 2 * DVE_UNITS.index(8) + b + 1)
                            av(YH[:, 2 + b, 0:t], cY[:, b, 0:t], ACT.Copy).then_inc(y_hi, 1)
                    act.wait_ge(s_max, 8 * l + s + 1)
                    for j in range(tiles(l)):
                        for q in range(2 if j == 2 else 1):
                            cs = slice(0, TOK) if j < 2 else slice(q * CTX, (q + 1) * CTX)
                            av(T[:, j, cs], ps[4 + j][:, cs], ACT.Exp, bias=stat[:, 1, j + q:j + q + 1], scale=SCALE,
                               accum_out=stat[:, 2, j + q:j + q + 1]).then_inc(p_exp, 1)
                    nq = 4 if l == 0 else 2
                    av(stat[:, 3, 0:nq], stat[:, 1, 0:nq], ACT.Exp, bias=sinkP[:, h:h + 1]).then_inc(p_exp, 1)
                    hi(n0 + 2 * u + 3)
                    for j in range(tiles(l)):
                        act.wait_ge(pt_mm, tile_count(l, s, j))
                        av(PTH[:, j, :], ps[4 + j][:], ACT.Copy).then_inc(pt_hi, 1)
                    act.wait_ge(w_used, n0 + 2 * u + 2)
                    if s == 4:
                        act.wait_ge(y_lo, 4 * l + 4)
                    G = GA if s < 4 else GB
                    for b in range(2):
                        av(G[:, 2 * (s % 4) + b, 0:t], ps[2 * (u % 2) + b][:, 0:t], ACT.Tanh, scale=0.5
                           ).then_inc(proj_act, 1)
                    act.wait_ge(pv_mm, 8 * l + s + 1)
                    rows = slice((s % 2) * HD, (s % 2 + 1) * HD)
                    av(QH[rows, s // 2, 0:t], ps[7][rows, 0:t], ACT.Copy).then_inc(o_hi, 1)
                for n in range(FIRST["oa", l] + 2, FIRST["out", l] + 2):
                    hi(n)
                for m in range(DC):
                    act.wait_ge(ob_sum, 8 * l + m + 1)
                    av(hH[:, m, 0:t], GB[:, m, 0:t], ACT.Copy).then_inc(m_hi, 1)
                    if m in (3, 7):
                        hi(FIRST["out", l] + 2 + m // 4)
                for n in range(FIRST["out", l] + 4, FIRST["out", l] + DC + 2):
                    hi(n)

            hi(0)
            hi(1)
            act.wait_ge(vec_out, 1)
            act.wait_ge(vec_step, 1)
            av(cact[:].rearrange("p v k -> p (v k)"), VT[:, V_C:V_C + 16], ACT.Silu).then_inc(c_silu, 1)
            for l in range(DEPTH):
                norm_act(3 * l, FIRST["wi1", l])
                ffn_act(2 * l, 3 * l)
                norm_act(3 * l + 1, FIRST["proj", l])
                mixers_act(l)
                norm_act(3 * l + 2, FIRST["wi2", l])
                ffn_act(2 * l + 1, 3 * l + 2)
            norm_act(6, 0)

        @block.vector
        def _(dve):
            tt, ts, stt = nc.vector.tensor_tensor, nc.vector.tensor_scalar, nc.vector.scalar_tensor_tensor
            steps = [0]

            def mark(ins):
                steps[0] += 1
                ins.then_inc(vec_step, 1)

            def settle():
                dve.wait_ge(vec_step, steps[0])

            def lo(n0, j=0, i=0):
                s = (n0 + j) % RING
                if n0 + j >= PIECES and isinstance(i, int):
                    return
                dve.wait_ge(hi_done, n0 + j + 1 if isinstance(i, int) else i * 4 + (n0 + j + 1))
                tt(wL[:, s, :], raw[:, s, :], wH[:, s, :].bitcast(F32), ALU.subtract).then_inc(lo_done, 1)

            def rows_evac(base, i=None):
                dve.wait_ge(ada_used, 4 * (base + 1) if i is None else i * 4 + 4 * (base + 1))
                if i is not None or base > 0:
                    dve.wait_ge(ada_T, base if i is None else i + base)
                nc.vector.tensor_copy(rowS[:], ps[5][:]).then_inc(row_out, 1)

            def ada_evac(base, i=None):
                dve.wait_ge(ada_T, base + 1 if i is None else i + (base + 1))
                if i is None:
                    dst, bias = mod[:, base], VT[:, V_BADA + base * DC:V_BADA + (base + 1) * DC]
                else:
                    dst = mod[:, bass.ds(i + base, 1)].rearrange("p a k v -> p (a k) v")
                    bias = VT[:, bass.ds(i * DC + (V_BADA + base * DC), DC)]
                tt(dst, ps[6][:, 0:2 * DC].rearrange("p (k v) -> p k v", v=2),
                   bias.unsqueeze(2).broadcast_to([P, DC, 2]), ALU.add).then_inc(ada_out, 1)

            def norm_dve(v, n0):
                t = T_NORM[v]
                if v < 6:
                    mi = 9 * (v // 3) + 3 * (v % 3)
                    dve.wait_ge(ada_out, mi + 2)
                    mark(stt(normA[:, v], mod[:, mi + 1], 1.0,
                             VT[:, V_NORM + v * DC:V_NORM + (v + 1) * DC].unsqueeze(2).broadcast_to([P, DC, 2]),
                             ALU.add, ALU.mult))
                dve.wait_ge(rms, v + 1)
                mark(nc.vector.reciprocal(T[:, 3, 0:t], T[:, 2, 0:t]))
                settle()
                if v == 6:
                    for m in range(DC):
                        if m >= 2:
                            dve.wait_ge(fin_T, 2 * (m - 1))
                        stt(T[:, m % 2, 0:t], X[:, m, 0:t], VT[:, V_FIN + m:V_FIN + m + 1], T[:, 3, 0:t],
                            ALU.mult, ALU.mult).then_inc(fin_ready, 1)
                    return

                def scaled(m):
                    for hf in range(halves(t)):
                        cs = slice(hf * SEQ, (hf + 1) * SEQ)
                        stt(T[:, m % 2, cs], X[:, m, cs], normA[:, v, m, hf:hf + 1], T[:, 3, cs],
                            ALU.mult, ALU.mult).then_inc(hp_done, 1)

                def low(m):
                    for hf in range(halves(t)):
                        cs = slice(hf * SEQ, (hf + 1) * SEQ)
                        dve.wait_ge(h_hi, h_count(v, m) - halves(t) + hf + 1)
                        stt(hL[:, m, cs], T[:, m % 2, cs], mod[:, mi, m, hf:hf + 1], hH[:, m, cs].bitcast(F32),
                            ALU.add, ALU.subtract).then_inc(h_lo, 1)
                scaled(0)
                for m in range(DC):
                    if m + 1 < DC:
                        if m >= 1:
                            dve.wait_ge(h_lo, h_count(v, m - 1))
                        scaled(m + 1)
                    low(m)
                    if m == 3:
                        lo(n0 + 2)
                    if m == 6:
                        lo(n0 + 3)

            def residual(r):
                t = T_AFTER[r]
                l, q = (r - 1) // 3, (r - 1) % 3
                mi = 9 * l + 3 * q + 2
                dve.wait_ge(ada_out, mi + 1)
                mark(ts(gateH[:, r - 1], mod[:, mi], 0.5, None, ALU.mult))
                settle()
                for m in range(DC):
                    wait_chunk(dve, l, ("wo1", "out", "wo2")[q], m)
                    for hf in range(halves(t)):
                        cs = slice(hf * SEQ, (hf + 1) * SEQ)
                        stt(X[:, m, cs], ps[bank_of(m)][:, cs], gateH[:, r - 1, m, hf:hf + 1], X[:, m, cs],
                            ALU.mult, ALU.add).then_inc(x_ready, 1)

            def product(f, t, i):
                for b in range(2):
                    dve.wait_ge(g_silu, i * 2 + (2 * GROUPS * f + b + 1))
                    dve.wait_ge(a_out, i * 2 + (2 * GROUPS * f + b + 1))
                    tt(T[:, 2 + b, 0:t], T[:, 2 + b, 0:t], T[:, b, 0:t], ALU.mult).then_inc(g_prod, 1)
                for b in range(2):
                    dve.wait_ge(g_hi, i * 2 + (2 * GROUPS * f + b + 1))
                    if isinstance(i, int):
                        high, low = GH[:, 2 * i + b, 0:t], GL[:, 2 * i + b, 0:t]
                    else:
                        high = GH[:, bass.ds(i * 2 + b, 1), 0:t].rearrange("p a t -> p (a t)")
                        low = GL[:, bass.ds(i * 2 + b, 1), 0:t].rearrange("p a t -> p (a t)")
                    tt(low, T[:, 2 + b, 0:t], high.bitcast(F32), ALU.subtract).then_inc(g_lo, 1)

            def ffn_dve(f, v):
                l, name = f // 2, "12"[f % 2]
                t = T_NORM[v]
                n0 = FIRST["wi" + name, l]
                if f == 1:
                    nc.vector.memset(ps[5][:], 0.0).then_inc(bank5_zero, 1)

                def group(i, ada0=None):
                    if ada0 is not None:
                        rows_evac(ada0 - 1, i)
                    lo(n0, 2, i)
                    lo(n0, 3, i)
                    product(f, t, i - 1)
                    if ada0 is not None:
                        ada_evac(ada0 - 1, i)
                    lo(n0, 4, i)
                    lo(n0, 5, i)
                lo(n0, 4)
                lo(n0, 5)
                ada0, count = ADA_IN_FFN.get(f, (None, 0))
                if count:
                    with dve.Fori(1, count + 1) as i:
                        group(i, ada0)
                if count + 1 < GROUPS - 1:
                    with dve.Fori(count + 1, GROUPS - 1) as i:
                        group(i)
                i = GROUPS - 1
                lo(n0 + 4 * i + 2)
                lo(n0 + 4 * i + 3)
                product(f, t, i - 1)
                lo(n0 + 4 * i + 4)
                lo(n0 + 4 * i + 5)
                product(f, t, i)
                n0 = FIRST["wo" + name, l]
                with dve.Fori(0, FC // RING) as i:
                    for j in range(RING):
                        lo(n0, 2 + j, i)
                for j in range(FC // RING * RING, FC):
                    lo(n0 + 2 + j)

            def rope_dve(l, bis):
                t = TOK if l == 0 else SEQ
                for bi in bis:
                    dve.wait_ge(rope_mm, 5 * l + bi + 1)
                    w = T[:, bi % 4, 0:SEQ]
                    mark(tt(ropeT[:, bi % 2, :], ps[4 + bi % 2][:, 0:SEQ], sinT, ALU.mult))
                    mark(tt(w, w, cosT, ALU.mult))
                    settle()
                    tt(w, w, ropeT[:, bi % 2, :], ALU.add).then_inc(rope_done, 1)
                for bi in bis:
                    dve.wait_ge(q_hi, 5 * l + bi + 1)
                    if bi < 4:
                        tt(QL[:, bi, 0:t], T[:, bi, 0:t], QH[:, bi, 0:t].bitcast(F32), ALU.subtract).then_inc(q_lo, 1)
                    else:
                        tt(KL[:], T[:, 0, :], KH[:].bitcast(F32), ALU.subtract).then_inc(q_lo, 1)

            def conv_taps(l, pair):
                segs = 2 if l == 0 else 1
                for k in range(CONV_K):
                    for b in range(2):
                        tap = VT[:, V_CONV + (l * CONV_K + k) * CC + 2 * pair + b:][:, 0:1]
                        src = cU[:, b, 0:segs, k:k + SEQ]
                        dst = cY[:, b, 0:segs * SEQ].rearrange("p (s t) -> p s t", s=segs)
                        if k == 0:
                            mark(ts(dst, src, tap, None, ALU.mult))
                        else:
                            mark(stt(dst, src, tap, dst, ALU.mult, ALU.add))
                    settle()

            def y_low(l, pair, t):
                for b in range(2):
                    dve.wait_ge(y_hi, 4 * l + 2 * pair + b + 1)
                    tt(YL[:, 2 * pair + b, 0:t], cY[:, b, 0:t], YH[:, 2 * pair + b, 0:t].bitcast(F32),
                       ALU.subtract).then_inc(y_lo, 1)

            def mixers_dve(l):
                t = TOK if l == 0 else SEQ
                segs = t // SEQ
                n0 = FIRST["proj", l]
                mark(nc.vector.memset(cU[:].rearrange("p a b c -> p (a b c)"), 0.0))
                settle()
                for u in range(9):
                    kind = UNITS[u]
                    pair = int(kind[1]) if kind != "kv" else 0
                    if u > 0:
                        lo(n0 + 2 * u + 2)
                        lo(n0 + 2 * u + 3)
                    if u in (1, 2):
                        rope_dve(l, (2 * u - 2, 2 * u - 1))
                    if u == 3:
                        rope_dve(l, (4,))
                        dve.wait_ge(v_hi, l + 1)
                        tt(VL[:].rearrange("p b d -> p (b d)"), ps[6][:],
                           VH[:].rearrange("p b d -> p (b d)").bitcast(F32), ALU.subtract).then_inc(v_lo, 1)
                    if u == 6:
                        y_low(l, 0, t)
                    if kind[0] == "u":
                        dve.wait_ge(w_used, n0 + 2 * u + 2)
                        dve.wait_ge(proj_act, 26 * l + 2 * ACT_UNITS.index(u - 1) + 2)
                        for b in range(2):
                            ins = tt(cU[:, b, 0:segs, 1:SEQ + 1],
                                     ps[2 * (u % 2) + b][:, 0:t].rearrange("p (s t) -> p s t", s=segs),
                                     cC[:, b, 0:t].rearrange("p (s t) -> p s t", s=segs), ALU.mult)
                            ins.then_inc(proj_dve, 1)
                        dve.wait_ge(proj_dve, 8 * l + 2 * DVE_UNITS.index(u) + 2)
                        conv_taps(l, pair)
                    if kind[0] == "b":
                        dve.wait_ge(w_used, n0 + 2 * u + 2)
                        for b in range(2):
                            w = cY[:, b, 0:t]
                            tt(w, ps[2 * (u % 2) + b][:, 0:t], w, ALU.mult).then_inc(proj_dve, 1)
                for s in range(8):
                    u = 9 + s
                    h = HEADS * l + STEP_HEAD[s]
                    nq = 4 if l == 0 else 2
                    lo(n0 + 2 * u + 2)
                    if s == 0:
                        y_low(l, 1, t)
                    dve.wait_ge(s_mm, tile_count(l, s, 0))
                    mark(tt(ps[4][:, P:2 * P], ps[4][:, P:2 * P], mask0, ALU.add))
                    dve.wait_ge(s_mm, tile_count(l, s, 1))
                    mark(tt(ps[5][:, 0:P], ps[5][:, 0:P], mask1, ALU.add))
                    settle()
                    for j in range(2):
                        mark(nc.vector.tensor_reduce(stat[:, 0, j:j + 1], ps[4 + j][:], AX_X, ALU.max))
                    if l == 0:
                        dve.wait_ge(s_mm, tile_count(l, s, 2))
                        mark(nc.vector.tensor_reduce(stat[:, 0, 2:4], ps[6][:].rearrange("p (q k) -> p q k", q=2),
                                                     AX_X, ALU.max))
                    settle()
                    ts(stat[:, 1, 0:nq], stat[:, 0, 0:nq], -SCALE, sinkN[:, h:h + 1], ALU.mult, ALU.min
                       ).then_inc(s_max, 1)
                    lo(n0 + 2 * u + 3)
                    dve.wait_ge(p_exp, (nq + 1) * (s + 1) + (40 if l else 0))
                    mark(tt(stat[:, 4, 0:nq], stat[:, 2, 0:nq], stat[:, 3, 0:nq], ALU.add))
                    settle()
                    mark(nc.vector.reciprocal(stat[:, 5, 0:nq], stat[:, 4, 0:nq]))
                    settle()
                    for j in range(tiles(l)):
                        for q in range(2 if j == 2 else 1):
                            cs = slice(0, TOK) if j < 2 else slice(q * CTX, (q + 1) * CTX)
                            ins = ts(T[:, j, cs], T[:, j, cs], stat[:, 5, j + q:j + q + 1], None, ALU.mult)
                            if j == 2 and q == 0:
                                mark(ins)
                                settle()
                            else:
                                ins.then_inc(p_norm, 1)
                    for j in range(tiles(l)):
                        dve.wait_ge(pt_hi, tile_count(l, s, j))
                        tt(PTL[:, j, :], ps[4 + j][:], PTH[:, j, :].bitcast(F32), ALU.subtract).then_inc(pt_lo, 1)
                    dve.wait_ge(o_hi, 8 * l + s + 1)
                    rows = slice((s % 2) * HD, (s % 2 + 1) * HD)
                    tt(QL[rows, s // 2, 0:t], ps[7][rows, 0:t], QH[rows, s // 2, 0:t].bitcast(F32),
                       ALU.subtract).then_inc(o_lo, 1)
                for n in range(FIRST["oa", l] + 2, FIRST["oa", l] + 6):
                    lo(n)
                for m in range(DC):
                    wait_chunk(dve, l, "oa", m)
                    stt(GA[:, m, 0:t], GA[:, m, 0:t], 1.0, ps[bank_of(m)][:, 0:t], ALU.add, ALU.mult
                        ).then_inc(oa_out, 1)
                for n in range(FIRST["ob", l] + 2, FIRST["ob", l] + 6):
                    lo(n)
                for m in range(DC):
                    wait_chunk(dve, l, "ob", m)
                    stt(GB[:, m, 0:t], GB[:, m, 0:t], 1.0, ps[bank_of(m)][:, 0:t], ALU.add, ALU.mult
                        ).then_inc(ob_out, 1)
                dve.wait_ge(oa_out, 8 * (l + 1))

                def branch_sum(m):
                    dve.wait_ge(ob_out, 8 * l + m + 1)
                    tt(GB[:, m, 0:t], GB[:, m, 0:t], GA[:, m, 0:t], ALU.add).then_inc(ob_sum, 1)
                branch_sum(0)
                for m in range(DC):
                    if m + 1 < DC:
                        branch_sum(m + 1)
                    dve.wait_ge(m_hi, 8 * l + m + 1)
                    tt(hL[:, m, 0:t], GB[:, m, 0:t], hH[:, m, 0:t].bitcast(F32), ALU.subtract).then_inc(m_lo, 1)
                    if m in (3, 7):
                        lo(FIRST["out", l] + 2 + m // 4)
                for n in range(FIRST["out", l] + 4, FIRST["out", l] + DC + 2):
                    lo(n)

            nc.vector.memset(ps[5][:], 0.0).then_inc(bank5_zero, 1)
            lo(0)
            lo(1)
            dve.wait_ge(vec_T, 1)
            nc.vector.tensor_copy(VT[:], ps[6][:, 0:NVEC]).then_inc(vec_out, 1)
            mark(nc.vector.memset(epsT[:], EPS))
            dve.wait_ge(in_sink, 16)
            mark(ts(sinkN[:], sinkP[:], -1.0, None, ALU.mult))
            for m in range(DC):
                dve.wait_ge(x_T, m + 1)
                nc.vector.tensor_copy(X[:, m, :], ps[m % 4][:]).then_inc(x_ready, 1)
            dve.wait_ge(vec_out, 1)
            for j in range(2):
                rows_evac(j)
                ada_evac(j)
            for l in range(DEPTH):
                norm_dve(3 * l, FIRST["wi1", l])
                ffn_dve(2 * l, 3 * l)
                residual(3 * l + 1)
                norm_dve(3 * l + 1, FIRST["proj", l])
                mixers_dve(l)
                residual(3 * l + 2)
                norm_dve(3 * l + 2, FIRST["wi2", l])
                ffn_dve(2 * l + 1, 3 * l + 2)
                residual(3 * l + 3)
            norm_dve(6, 0)
            for tb in range(2):
                for half in range(2):
                    dve.wait_ge(fin_T, 2 * DC if half else DC - 1 + tb)
                    nc.vector.tensor_copy(yout[:, tb, half * TOK:(half + 1) * TOK], ps[2 * tb + half][:]
                                          ).then_inc(fin_out, 1)


_INS = ["x", "c", "ctx", "c_ctx", "w_ada", "b_ada", "norm_w", "ffn1_wi", "ffn1_wo", "w_in", "conv_w", "sink", "w_oa",
        "w_ob", "w_out", "ffn2_wi", "ffn2_wo", "final_norm_w"]


def kernel(**inputs):
    import concourse.bacc as bacc
    from concourse.bass_utils import run_bass_kernel_spmd

    nc = bacc.Bacc("TRN2", target_bir_lowering=False, num_devices=1)
    arrays, args = {}, []
    for name in _INS + ["shape_consts"]:
        a = shape_constants() if name == "shape_consts" else np.ascontiguousarray(inputs[name])
        arrays[f"in_{name}"] = a
        args.append(nc.dram_tensor(f"in_{name}", a.shape, mybir.dt.from_np(a.dtype), kind="ExternalInput").ap())
    args.append(nc.dram_tensor("out", (1, SEQ, D), F32, kind="ExternalOutput").ap())
    build(nc, *args)
    r = run_bass_kernel_spmd(nc, [arrays], core_ids=[0])
    return r.results[0]["out"]
```

```python
from contextlib import ExitStack

import numpy as np

import concourse.bass as bass
from concourse import mybir

P = 128
F32 = mybir.dt.float32
F32R = mybir.dt.float32r
ALU = mybir.AluOpType
ACT = mybir.ActivationFunctionType
AX_X = mybir.AxisListType.X

D = 1024
DC = D // P
SEQ = 256
CTX = 256
TOK = SEQ + CTX
DEPTH = 2
NMOD = 9
HEADS, KV_HEADS, HD = 8, 2, 64
ATTN_W, KV_W, CONV_W = HEADS * HD, KV_HEADS * HD, D // 2
CC = CONV_W // P
CONV_K = 3
WINDOW = 128
GRID_W = 64
DFF = 2816
FC = DFF // P
GROUPS = FC // 2
EPS = 1e-6
SCALE = HD ** -0.5
NEG = -1e30

Q0 = 0
K0 = ATTN_W
B0 = ATTN_W + 2 * KV_W
C0 = B0 + CONV_W
U0 = C0 + CONV_W
GA0 = U0 + CONV_W
GB0 = GA0 + D

RING = 4
PIECE = 8 * P

V_NORM, V_CONV, V_FIN, V_C = 0, 48, 72, 80
V_BADA = 96
NVEC = V_BADA + DEPTH * NMOD * DC


def shape_constants():
    d = np.arange(P) % HD
    t = np.arange(SEQ)
    pos = np.where((d < HD // 2)[:, None], (t // GRID_W)[None, :], (t % GRID_W)[None, :]).astype(np.float32)
    inv = (np.float32(10000.0) ** (-(d % (HD // 4)).astype(np.float32) / np.float32(HD // 4))).astype(np.float32)
    ang = (pos * inv[:, None]).astype(np.float32)
    rot = np.zeros((P, P))
    for i in range(P):
        if i % (HD // 2) < HD // 4:
            rot[i + HD // 4, i] = -1.0
        else:
            rot[i - HD // 4, i] = 1.0
    q, k = np.arange(P)[:, None], np.arange(P)[None, :]
    return np.concatenate([np.cos(ang), np.sin(ang), rot, np.eye(P), np.full((P, P), 1.0 / D),
                           np.where(k <= q, 0.0, NEG), np.where(k >= q, 0.0, NEG)], axis=1).astype(np.float32)


N_CONST = 2 * SEQ + 5 * P

WI_P, WO_P, OA_P, OB_P, OUT_P = 4 * GROUPS, FC, CC, CC, DC
UNITS = ["kv", "q0", "q1", "c0", "u0", "b0", "c1", "u1", "b1"] + [f"g{i}" for i in range(8)]
PROJ_P = 2 * len(UNITS)
ACT_UNITS = [u for u, k in enumerate(UNITS) if k[0] in "qkcg"]
DVE_UNITS = [u for u, k in enumerate(UNITS) if k[0] in "ub"]


def piece_plan():
    first, n, ways = {}, 0, []
    for l in range(DEPTH):
        for name, count in (("wi1", WI_P), ("wo1", WO_P), ("proj", PROJ_P), ("oa", OA_P), ("ob", OB_P),
                            ("out", OUT_P), ("wi2", WI_P), ("wo2", WO_P)):
            first[name, l] = n
            ways += [4 if name == "proj" and 2 <= j < 6 else 2 if name == "oa" else 1 for j in range(count)]
            n += count
    at, loaded = [0] * RING, []
    for j, w in enumerate(ways):
        at[j % RING] += 16 * w
        loaded.append(at[j % RING])
    return first, loaded, n


FIRST, LOADED, PIECES = piece_plan()
ADA_IN_FFN = {0: (2, 7), 1: (9, 9)}
HEAD0 = 8
STEP_HEAD = [b + 4 * r for b in range(4) for r in range(2)]


def bank_of(m):
    return (m + 4) % 8


def build(nc, x, c, ctx, c_ctx, w_ada, b_ada, norm_w, ffn1_wi, ffn1_wo, w_in, conv_w, sink, w_oa, w_ob, w_out,
          ffn2_wi, ffn2_wo, final_norm_w, consts, out):
    stack = ExitStack()
    with stack:
        def sb(name, shape, dt=F32):
            return stack.enter_context(nc.sbuf_tensor(name, shape, dt))

        def sem(name):
            return stack.enter_context(nc.semaphore(name))

        X = sb("X", [P, DC, TOK])
        hH = sb("hH", [P, DC, TOK], F32R)
        with ExitStack() as s:
            adaC = s.enter_context(nc.sbuf_tensor("adaC", [P, 4, D], F32))
        hL = sb("hL", [P, DC, TOK], F32R)
        raw = sb("raw", [P, RING, PIECE])
        wH = sb("wH", [P, RING, PIECE], F32R)
        wL = sb("wL", [P, RING, PIECE], F32R)
        T = sb("T", [P, 4, TOK])
        cst = sb("cst", [P, N_CONST])
        VT = sb("VT", [P, NVEC])
        mod = sb("mod", [P, DEPTH * NMOD, DC, 2])
        normA = sb("normA", [P, 3 * DEPTH, DC, 2])
        gateH = sb("gateH", [P, 3 * DEPTH, DC, 2])
        cact = sb("cact", [P, 2, DC])
        sinkP = sb("sinkP", [P, DEPTH * HEADS])
        sinkN = sb("sinkN", [P, DEPTH * HEADS])
        epsT = sb("epsT", [P, 1])
        root = sb("root", [P, 2, 8])
        stat = sb("stat", [P, 6, 4])
        with ExitStack() as r:
            adaA = r.enter_context(nc.sbuf_tensor("adaA", [P, 2, D], F32))
            with ExitStack() as s:
                GH = s.enter_context(nc.sbuf_tensor("GH", [P, FC, TOK], F32R))
                GL = s.enter_context(nc.sbuf_tensor("GL", [P, FC, TOK], F32R))
            with ExitStack() as s:
                s.enter_context(nc.sbuf_tensor("hidden_front", [P, FC - 4, TOK], F32))
                rowS = s.enter_context(nc.sbuf_tensor("rowS", [P, TOK], F32))
                s.enter_context(nc.sbuf_tensor("hidden_mid", [P, 3 + FC - 4, TOK], F32))
                adaB = s.enter_context(nc.sbuf_tensor("adaB", [P, 2, D], F32))
            with ExitStack() as s:
                def mb(name, shape, dt=F32):
                    return s.enter_context(nc.sbuf_tensor(name, shape, dt))
                QH = mb("QH", [P, 4, TOK], F32R)
                QL = mb("QL", [P, 4, TOK], F32R)
                KH = mb("KH", [P, TOK], F32R)
                KL = mb("KL", [P, TOK], F32R)
                V32 = mb("V32", [P, TOK])
                VH = mb("VH", [P, 4, P], F32R)
                VL = mb("VL", [P, 4, P], F32R)
                YH = mb("YH", [P, CC, TOK], F32R)
                YL = mb("YL", [P, CC, TOK], F32R)
                GA = mb("GA", [P, DC, TOK])
                PTH = mb("PTH", [P, 3, TOK], F32R)
                PTL = mb("PTL", [P, 3, TOK], F32R)
                with ExitStack() as s2:
                    GB = s2.enter_context(nc.sbuf_tensor("GB", [P, DC, TOK], F32))
                cC = mb("cC", [P, 2, TOK])
                cU = mb("cU", [P, 2, 2, SEQ + 2])
                cY = mb("cY", [P, 2, TOK])
                ropeT = mb("ropeT", [P, 2, SEQ])
            with ExitStack() as s:
                xin = s.enter_context(nc.sbuf_tensor("xin", [P, 4, D], F32))
                vin = s.enter_context(nc.sbuf_tensor("vin", [P, 3, P], F32))
                ada0a = s.enter_context(nc.sbuf_tensor("ada0a", [P, 4, D], F32))
                s.enter_context(nc.sbuf_tensor("around_rows", [P, 9, P], F32))
                ada0b = s.enter_context(nc.sbuf_tensor("ada0b", [P, 8, D], F32))
            with ExitStack() as s:
                yout = s.enter_context(nc.sbuf_tensor("yout", [P, 2, D], F32))
        ps = [stack.enter_context(nc.psum_tensor(f"ps{i}", [P, TOK], F32)) for i in range(8)]

        cosT, sinT = cst[:, 0:SEQ], cst[:, SEQ:2 * SEQ]
        o = 2 * SEQ
        ada0 = [ada0a[:, k] for k in range(4)] + [ada0b[:, k] for k in range(8)] + [adaC[:, k] for k in range(4)]
        ada = [adaA[:, 0], adaA[:, 1], adaB[:, 0], adaB[:, 1]]
        rotM, ident, meanM, mask0, mask1 = (cst[:, o + j * P:o + (j + 1) * P] for j in range(5))

        loaded = [sem(f"loaded{i}") for i in range(RING)]
        hi_done = sem("hi_done")
        lo_done = sem("lo_done")
        w_used = sem("w_used")
        in_vec, in_x, in_c, in_sink = sem("in_vec"), sem("in_x"), sem("in_c"), sem("in_sink")
        ada0_loaded = [sem(f"ada0_loaded{i}") for i in range(4)]
        ada_loaded = [sem(f"ada_loaded{i}") for i in range(4)]
        ada_used = sem("ada_used")
        bank5_zero = sem("bank5_zero")
        row_out = sem("row_out")
        ada_T = sem("ada_T")
        ada_part = sem("ada_part")
        ada_out = sem("ada_out")
        vec_T, vec_out, c_silu = sem("vec_T"), sem("vec_out"), sem("c_silu")
        x_T = sem("x_T")
        x_ready = sem("x_ready")
        sq_done, sq_used = sem("sq_done"), sem("sq_used")
        rms = sem("rms")
        rms_diag = sem("rms_diag")
        rms_row = sem("rms_row")
        hp_done = sem("hp_done")
        h_hi, h_lo = sem("h_hi"), sem("h_lo")
        a_out, g_silu = sem("a_out"), sem("g_silu")
        g_prod, g_hi, g_lo = sem("g_prod"), sem("g_hi"), sem("g_lo")
        acc_mm = sem("acc_mm")
        oa_out, ob_out, ob_sum = sem("oa_out"), sem("ob_out"), sem("ob_sum")
        m_hi, m_lo = sem("m_hi"), sem("m_lo")
        proj_act, proj_dve = sem("proj_act"), sem("proj_dve")
        rope_mm, rope_done, q_hi, q_lo = sem("rope_mm"), sem("rope_done"), sem("q_hi"), sem("q_lo")
        v_T, v_hi, v_lo = sem("v_T"), sem("v_hi"), sem("v_lo")
        y_hi, y_lo = sem("y_hi"), sem("y_lo")
        s_mm, s_max, p_exp, p_norm = sem("s_mm"), sem("s_max"), sem("p_exp"), sem("p_norm")
        pt_mm, pt_hi, pt_lo = sem("pt_mm"), sem("pt_hi"), sem("pt_lo")
        pv_mm, o_hi, o_lo = sem("pv_mm"), sem("o_hi"), sem("o_lo")
        vec_step = sem("vec_step")
        fin_ready, fin_T, fin_out, stored = sem("fin_ready"), sem("fin_T"), sem("fin_out"), sem("stored")

        def wait(eng, s, v):
            if not isinstance(v, int) or v > 0:
                eng.wait_ge(s, v)

        T_AFTER = [TOK, TOK, TOK, TOK, TOK, SEQ, SEQ]
        T_NORM = [TOK, TOK, TOK, TOK, TOK, SEQ, SEQ]

        def halves(t):
            return t // SEQ

        def x_count(r, m):
            n = sum(DC * (1 if q == 0 else halves(T_AFTER[q])) for q in range(r))
            return n + (m + 1) * (1 if r == 0 else halves(T_AFTER[r]))

        def h_count(v, m):
            return sum(DC * halves(T_NORM[q]) for q in range(v)) + (m + 1) * halves(T_NORM[v])

        def tiles(l):
            return 3 if l == 0 else 2

        def tile_count(l, s, j):
            return (0 if l == 0 else 8 * 3) + s * tiles(l) + j + 1

        def wait_chunk(eng, l, name, m):
            idx = ("wo1", "oa", "ob", "out", "wo2").index(name)
            if m < DC - 1:
                eng.wait_ge(acc_mm, (DC - 1) * (5 * l + idx) + m + 1)
            else:
                pieces = {"wo1": WO_P, "oa": OA_P, "ob": OB_P, "out": OUT_P, "wo2": WO_P}[name]
                eng.wait_ge(w_used, FIRST[name, l] + pieces)

        block = stack.enter_context(nc.Block())

        @block.sync
        def _(sp):
            sp.dma_start(vin[0:48, 0, :], norm_w.rearrange("l j (k p) -> (l j k) p", p=P)).then_inc(in_vec, 16)
            sp.dma_start(vin[V_CONV:72, 0, :], conv_w.rearrange("l j (k p) -> (l j k) p", p=P)).then_inc(in_vec, 16)
            sp.dma_start(vin[V_FIN:80, 0, :], final_norm_w.rearrange("(k p) -> k p", p=P)).then_inc(in_vec, 16)
            sp.dma_start(vin[V_C:88, 0, :], c.rearrange("b (k p) -> (b k) p", p=P)).then_inc(in_vec, 16)
            sp.dma_start(vin[88:96, 0, :], c_ctx.rearrange("(k p) -> k p", p=P)).then_inc(in_vec, 16)
            for l in range(DEPTH):
                sp.dma_start(vin[0:NMOD * DC, 1 + l, :],
                             b_ada[l].rearrange("(k p) -> k p", p=P)).then_inc(in_vec, 16)
            sp.dma_start(cst[:], consts).then_inc(in_c, 16)
            sp.dma_start(xin[:, 0:2, :], x[0].rearrange("(t p) d -> p t d", p=P)).then_inc(in_x, 16)
            sp.dma_start(xin[:, 2:4, :], ctx[0].rearrange("(t p) d -> p t d", p=P)).then_inc(in_x, 16)
            for i, dst in enumerate((ada0a[:], ada0b[:, 0:4], ada0b[:, 4:8], adaC[:])):
                sp.dma_start(dst, w_ada[0].rearrange("(k p) n -> p k n", p=P)[:, 4 * (i % 2):4 * (i % 2) + 4,
                                                                              (i // 2) * D:(i // 2 + 1) * D]
                             ).then_inc(ada0_loaded[i], 16)
            sp.dma_start(sinkP[:], sink.rearrange("l h -> (l h)").partition_broadcast(P)).then_inc(in_sink, 16)

            def slot_free(n0, j, i=0):
                if isinstance(i, int):
                    wait(sp, lo_done, n0 + j + 4 * i - RING + 1)
                else:
                    sp.wait_ge(lo_done, i * 4 + (n0 + j - RING + 1))

            def load_columns(n0, j, src, kh, col, i=0):
                slot_free(n0, j, i)
                s = (n0 + j) % RING
                sp.dma_start(raw[:, s, :].rearrange("p (k n) -> p k n", k=4),
                             src.rearrange("(k p) n -> p k n", p=P)[:, 4 * kh:4 * kh + 4, bass.ds(col, 2 * P)]
                             ).then_inc(loaded[s], 16)

            def load_rows(n0, j, src, k, i=0):
                slot_free(n0, j, i)
                s = (n0 + j) % RING
                sp.dma_start(raw[:, s, :], src[bass.ds(k * P, P), :]).then_inc(loaded[s], 16)

            def ffn_loads(l, name, wi, wo):
                n0 = FIRST["wi" + name, l]

                def group(i):
                    for j in range(4):
                        load_columns(n0, j, wi, j % 2, i * (2 * P) + (j // 2) * DFF, i)
                group(0)
                with sp.Fori(1, GROUPS) as i:
                    group(i)
                n0 = FIRST["wo" + name, l]
                with sp.Fori(0, FC // RING) as i:
                    for j in range(RING):
                        load_rows(n0, j, wo, i * RING + j, i)
                for j in range(FC // RING * RING, FC):
                    load_rows(n0, j, wo, j)

            for l in range(DEPTH):
                ffn_loads(l, "1", ffn1_wi[l], ffn1_wo[l])
                n0 = FIRST["proj", l]
                wv = w_in[l].rearrange("(k p) n -> p k n", p=P)
                for u, kind in enumerate(UNITS[:9]):
                    i = int(kind[1]) if kind != "kv" else 0
                    for kh in range(2):
                        if kind[0] == "q":
                            n = n0 + 2 * u + kh
                            slot_free(n, 0)
                            dst = raw[:, n % RING, :].rearrange("p (k b r d) -> p k b r d", k=4, b=2, r=2)
                            for b in range(2):
                                for r in range(2):
                                    col = Q0 + (2 * i + b + 4 * r) * HD
                                    sp.dma_start(dst[:, :, b, r, :], wv[:, 4 * kh:4 * kh + 4, col:col + HD]
                                                 ).then_inc(loaded[n % RING], 16)
                        else:
                            col = {"k": K0, "b": B0, "c": C0, "u": U0}[kind[0]] + 2 * P * i
                            load_columns(n0 + 2 * u + kh, 0, w_in[l], kh, col)
                with sp.Fori(0, 4) as i:
                    for j in range(4):
                        load_columns(n0 + 18, j, w_in[l], j % 2, i * (4 * P) + (j // 2) * 2 * P + GA0, i)
                for b in range(4):
                    n = FIRST["oa", l] + b
                    slot_free(n, 0)
                    for r in range(2):
                        sp.dma_start(raw[r * HD:(r + 1) * HD, n % RING, :],
                                     w_oa[l, (b + 4 * r) * HD:(b + 4 * r + 1) * HD, :]).then_inc(loaded[n % RING], 16)
                for k in range(4):
                    load_rows(FIRST["ob", l], k, w_ob[l], k)
                for k in range(DC):
                    load_rows(FIRST["out", l], k, w_out[l], k)
                ffn_loads(l, "2", ffn2_wi[l], ffn2_wo[l])
            for tb in range(2):
                sp.wait_ge(fin_out, 2 * tb + 2)
                sp.dma_start(out[0, tb * P:(tb + 1) * P, :], yout[:, tb, :]).then_inc(stored, 16)
            sp.wait_ge(stored, 32)

        @block.gpsimd
        def _(pool):
            def load_ada(mi, k, base, i=None):
                l, j = mi
                need = 4 * base + k // 2 - 1
                if i is None:
                    wait(pool, ada_used, need)
                    src = w_ada[l, k * P:(k + 1) * P, j * D:(j + 1) * D]
                else:
                    pool.wait_ge(ada_used, i * 4 + need)
                    src = w_ada[l, k * P:(k + 1) * P, bass.ds(i * D + j * D, D)]
                pool.dma_start(ada[k % 4], src).then_inc(ada_loaded[k % 4], 16)

            pool.wait_ge(ada0_loaded[3], 16)
            for k in range(4):
                pool.dma_start(ada[k], w_ada[0, k * P:(k + 1) * P, 2 * D:3 * D]).then_inc(ada_loaded[k], 16)
            for k in range(4, DC):
                load_ada((0, 2), k, 2)
            with pool.Fori(1, 7) as i:
                for k in range(DC):
                    load_ada((0, 2), k, 2, i)
            pool.wait_ge(m_lo, 8)
            with pool.Fori(0, NMOD) as i:
                for k in range(DC):
                    load_ada((1, 0), k, 9, i)

        @block.tensor
        def _(pe):
            mm = nc.tensor.matmul

            def triple(dst, wa, wb, ra, rb, start, stop, group_check=True):
                kw = {} if group_check else {"skip_group_check": True}
                mm(dst, wa, ra, start=start, stop=False, **kw)
                mm(dst, wa, rb, start=False, stop=False, **kw)
                return mm(dst, wb, ra, start=False, stop=stop, **kw)

            def ada_pair(p, base, i=None):
                for k in (2 * p, 2 * p + 1):
                    if base < 2:
                        pe.wait_ge(ada0_loaded[2 * base + k // 4], 16)
                        continue
                    count = 16 * (2 * (base - 2) + k // 4 + 1)
                    pe.wait_ge(ada_loaded[k % 4], count if i is None else i * 32 + count)
                if p == 0:
                    if i is None:
                        wait(pe, row_out, base)
                    else:
                        pe.wait_ge(row_out, i + base)
                for k in (2 * p, 2 * p + 1):
                    src = ada0[8 * base + k] if base < 2 else ada[k % 4]
                    for h in range(2):
                        g = 2 * (k % 2) + h
                        last = mm(ps[5][32 * g:32 * g + 2, :], cact[:, :, k], src[:, h * TOK:(h + 1) * TOK],
                                  start=(p == 0), stop=(p == 3), skip_group_check=True)
                last.then_inc(ada_used, 1)

            def ada_turn(base, i=None):
                pe.wait_ge(row_out, base + 1 if i is None else i + (base + 1))
                if i is None:
                    wait(pe, ada_out, base)
                else:
                    pe.wait_ge(ada_out, i + base)
                for q in range(4):
                    last = nc.tensor.transpose(ps[6][:, q * P:(q + 1) * P], rowS[:, q * P:(q + 1) * P], ident)
                last.then_inc(ada_T, 1)

            def columns_piece(n0, j, banks, kh, t, i=0, v=None):
                s = (n0 + j) % RING
                pe.wait_ge(lo_done, i * 4 + (n0 + j + 1))
                for k in range(4):
                    kk = 4 * kh + k
                    ws = [slice(k * 2 * P + b * P, k * 2 * P + (b + 1) * P) for b in range(2)]
                    if v is not None:
                        pe.wait_ge(h_hi, h_count(v, kk))
                        for b, w in enumerate(ws):
                            mm(ps[banks + b][:, 0:t], wH[:, s, w], hH[:, kk, 0:t], start=(kk == 0), stop=False,
                               skip_group_check=True)
                            mm(ps[banks + b][:, 0:t], wL[:, s, w], hH[:, kk, 0:t], start=False, stop=False,
                               skip_group_check=True)
                        pe.wait_ge(h_lo, h_count(v, kk))
                        for b, w in enumerate(ws):
                            last = mm(ps[banks + b][:, 0:t], wH[:, s, w], hL[:, kk, 0:t], start=False,
                                      stop=(kk == DC - 1), skip_group_check=True)
                        continue
                    for b, w in enumerate(ws):
                        last = triple(ps[banks + b][:, 0:t], wH[:, s, w], wL[:, s, w], hH[:, kk, 0:t], hL[:, kk, 0:t],
                                      kk == 0, kk == DC - 1, False)
                last.then_inc(w_used, 1)

            def rows_piece(n0, j, k, ra, rb, t, start, stop, i=0, bank_wait=None):
                s = (n0 + j) % RING
                pe.wait_ge(lo_done, i * 4 + (n0 + j + 1))
                for m in range(DC):
                    if bank_wait is not None:
                        bank_wait(m)
                    last = triple(ps[bank_of(m)][:, 0:t], wH[:, s, m * P:(m + 1) * P], wL[:, s, m * P:(m + 1) * P],
                                  ra[:, bass.ds(k, 1), 0:t].rearrange("p a t -> p (a t)") if not isinstance(k, int) else ra[:, k, 0:t],
                                  rb[:, bass.ds(k, 1), 0:t].rearrange("p a t -> p (a t)") if not isinstance(k, int) else rb[:, k, 0:t],
                                  start, stop, False)
                    if stop and m < DC - 1:
                        last.then_inc(acc_mm, 1)
                last.then_inc(w_used, 1)

            def mean_squares(v):
                t = T_NORM[v]
                wait(pe, x_ready, x_count(v, 0))
                for m in range(DC):
                    pe.wait_ge(sq_done, DC * v + m + 1)
                    for tb in range(t // P):
                        last = mm(ps[4][:, 2 * tb:2 * tb + 2], T[:, m % 2, tb * P:(tb + 1) * P], meanM[:, 0:2],
                                  start=(m == 0 and tb == 0), stop=(m == DC - 1), skip_group_check=True)
                    last.then_inc(sq_used, 1)

            def spread_roots(v):
                t = T_NORM[v]
                pe.wait_ge(rms_diag, sum(T_NORM[:v + 1]) // P)
                mm(ps[4][:, 0:t], meanM, T[:, 2, 0:t], start=True, stop=True).then_inc(rms_row, 1)

            def norm_pe(v):
                mean_squares(v)
                spread_roots(v)

            def ffn(f, v):
                l, name = f // 2, "12"[f % 2]
                t = T_NORM[v]
                n0 = FIRST["wi" + name, l]

                def group(i, ada_base=None, turn_base=None):
                    if isinstance(i, int) and i == 0:
                        wait(pe, x_ready, x_count(v, DC - 1))
                    else:
                        pe.wait_ge(a_out, i * 2 + 2 * GROUPS * f)
                    for j in range(4):
                        if j == 2 and not (isinstance(i, int) and i == 0):
                            pe.wait_ge(g_silu, i * 2 + 2 * GROUPS * f)
                        columns_piece(n0, j, 2 * (j // 2), j % 2, t, i,
                                      v if isinstance(i, int) and i == 0 and j < 2 else None)
                        if ada_base is not None:
                            if isinstance(i, int):
                                ada_pair(j, ada_base + i)
                            else:
                                ada_pair(j, ada_base, i)
                        if turn_base is not None and j == 0:
                            if isinstance(i, int):
                                ada_turn(turn_base + i - 1)
                            else:
                                ada_turn(turn_base - 1, i)

                ada0, count = ADA_IN_FFN.get(f, (None, 0))
                if count:
                    pe.wait_ge(bank5_zero, f + 1)
                group(0, ada0)
                if count:
                    with pe.Fori(1, count) as i:
                        group(i, ada0, ada0)
                    group(count, None, ada0)
                if count + 1 < GROUPS:
                    with pe.Fori(max(count, 0) + 1, GROUPS) as i:
                        group(i)
                n0 = FIRST["wo" + name, l]
                if count:
                    pe.wait_ge(ada_out, ada0 + count)

                def bank_wait(m):
                    if m == 4:
                        pe.wait_ge(a_out, 2 * GROUPS * (f + 1))
                    if m == 6:
                        pe.wait_ge(g_silu, 2 * GROUPS * (f + 1))
                pe.wait_ge(g_lo, 2 * GROUPS * (f + 1) - 2)
                for j in range(RING):
                    rows_piece(n0, j, j, GH, GL, t, j == 0, False, bank_wait=bank_wait if j == 0 else None)
                with pe.Fori(1, FC // RING) as i:
                    for j in range(RING):
                        rows_piece(n0, j, i * RING + j, GH, GL, t, False, False, i)
                pe.wait_ge(g_lo, 2 * GROUPS * (f + 1))
                for j in range(FC // RING * RING, FC):
                    rows_piece(n0, j, j, GH, GL, t, False, j == FC - 1)

            def rope(l, bi):
                o = (bi + 1) % 5
                pe.wait_ge(proj_act, 26 * l + (1 if bi == 4 else 3 + bi))
                if o >= 2:
                    pe.wait_ge(rope_done, 5 * l + o - 1)
                mm(ps[4 + o % 2][:, 0:SEQ], rotM, T[:, min(bi, 3), 0:SEQ], start=True, stop=True).then_inc(rope_mm, 1)

            def unit_banks_free(l, u):
                if u >= 2:
                    p = u - 2
                    if p in ACT_UNITS:
                        pe.wait_ge(proj_act, 26 * l + 2 * ACT_UNITS.index(p) + 2)
                    else:
                        pe.wait_ge(proj_dve, 8 * l + 2 * DVE_UNITS.index(p) + 2)

            def scores(l, s):
                b, r = s // 2, s % 2
                rows = slice(r * HD, (r + 1) * HD)
                if s == 0:
                    pe.wait_ge(q_lo, 5 * (l + 1))
                    pe.wait_ge(v_lo, l + 1)
                for j in range(tiles(l)):
                    if s > 0:
                        pe.wait_ge(pt_lo, tile_count(l, s - 1, j))
                    for q in range(2 if j == 2 else 1):
                        tq = j + q
                        qs = slice(tq * P, (tq + 1) * P)
                        keys = slice(0, TOK) if j < 2 else slice(SEQ, TOK)
                        dst = ps[4 + j][:, 0:TOK] if j < 2 else ps[6][:, q * CTX:(q + 1) * CTX]
                        last = triple(dst, QH[rows, b, qs], QL[rows, b, qs], KH[rows, keys], KL[rows, keys], True, True)
                    last.then_inc(s_mm, 1)

            def transpose_probs(l, s):
                for j in range(tiles(l)):
                    pe.wait_ge(p_norm, tile_count(l, s, j))
                    for q in range(4):
                        src = T[:, j, q * P:(q + 1) * P] if j < 2 else \
                            T[:, 2, (q % 2) * CTX + (q // 2) * P:(q % 2) * CTX + (q // 2 + 1) * P]
                        last = nc.tensor.transpose(ps[4 + j][:, q * P:(q + 1) * P], src, ident)
                    last.then_inc(pt_mm, 1)

            def weigh_values(l, s):
                pe.wait_ge(pt_lo, tile_count(l, s, tiles(l) - 1))
                if s > 0:
                    pe.wait_ge(o_lo, 8 * l + s)
                for kb in range(4):
                    ks = slice(kb * P, (kb + 1) * P)
                    last = triple(ps[7][:, 0:SEQ].rearrange("p (t q) -> p t q", t=2), VH[:, kb, :], VL[:, kb, :],
                                  PTH[:, 0:2, ks], PTL[:, 0:2, ks], kb == 0, kb == 3)
                if l == 0:
                    for kb in range(2):
                        ks = slice(kb * CTX, (kb + 1) * CTX)
                        last = triple(ps[7][:, SEQ:TOK], VH[:, 2 + kb, :], VL[:, 2 + kb, :],
                                      PTH[:, 2, ks], PTL[:, 2, ks], kb == 0, kb == 1)
                last.then_inc(pv_mm, 1)

            def mixers(l):
                v = 3 * l + 1
                t = TOK if l == 0 else SEQ
                n0 = FIRST["proj", l]
                pe.wait_ge(x_ready, x_count(v, DC - 1))
                for h in range(PROJ_P):
                    u, kh = h // 2, h % 2
                    if h == 3:
                        rope(l, 4)
                        pe.wait_ge(proj_act, 26 * l + 2)
                        for tb in range(4):
                            last = nc.tensor.transpose(ps[6][:, tb * P:(tb + 1) * P], V32[:, tb * P:(tb + 1) * P],
                                                       ident)
                        last.then_inc(v_T, 1)
                    if h in (5, 7):
                        rope(l, h - 5)
                        rope(l, h - 4)
                    s, stage = divmod(h - HEAD0, 3)
                    if stage == 0 and 1 <= s <= HEADS:
                        weigh_values(l, s - 1)
                    if stage == 0 and 0 <= s < HEADS:
                        scores(l, s)
                    if stage == 2 and 0 <= s < HEADS:
                        transpose_probs(l, s)
                    if kh == 0:
                        unit_banks_free(l, u)
                    columns_piece(n0 + h, 0, 2 * (u % 2), kh, TOK if UNITS[u] == "kv" else t, v=v if u == 0 else None)

                def oa_bank(m):
                    if m == 0:
                        pe.wait_ge(o_lo, 8 * (l + 1))
                        pe.wait_ge(proj_act, 26 * (l + 1))
                for k in range(4):
                    rows_piece(FIRST["oa", l] + k, 0, k, QH, QL, t, k == 0, k == 3, bank_wait=oa_bank if k == 0 else None)

                def ob_bank(m):
                    pe.wait_ge(oa_out, 8 * l + m + 1)
                pe.wait_ge(y_lo, 4 * (l + 1))
                for k in range(4):
                    rows_piece(FIRST["ob", l] + k, 0, k, YH, YL, t, k == 0, k == 3, bank_wait=ob_bank if k == 0 else None)

                def out_bank(m):
                    pe.wait_ge(ob_out, 8 * l + m + 1)
                for k in range(DC):
                    pe.wait_ge(m_lo, 8 * l + k + 1)
                    rows_piece(FIRST["out", l] + k, 0, k, hH, hL, t, k == 0, k == DC - 1,
                               bank_wait=out_bank if k == 0 else None)

            pe.wait_ge(in_c, 16)
            pe.wait_ge(in_vec, 16 * 7)
            nc.tensor.transpose(ps[6][:, 0:96], vin[0:96, 0, :], ident[0:96, 0:96])
            for l in range(DEPTH):
                last = nc.tensor.transpose(ps[6][:, 96 + 72 * l:96 + 72 * (l + 1)], vin[0:72, 1 + l, :],
                                           ident[0:72, 0:72])
            last.then_inc(vec_T, 1)
            pe.wait_ge(in_x, 32)
            for m in range(DC):
                if m >= 4:
                    pe.wait_ge(x_ready, m - 3)
                for tb in range(4):
                    last = nc.tensor.transpose(ps[m % 4][:, tb * P:(tb + 1) * P], xin[:, tb, m * P:(m + 1) * P], ident)
                last.then_inc(x_T, 1)
            mean_squares(0)
            pe.wait_ge(c_silu, 1)
            pe.wait_ge(bank5_zero, 1)
            pe.wait_ge(vec_out, 1)
            for j in range(2):
                for p in range(4):
                    ada_pair(p, j)
                ada_turn(j)
            spread_roots(0)

            for l in range(DEPTH):
                ffn(2 * l, 3 * l)
                norm_pe(3 * l + 1)
                mixers(l)
                norm_pe(3 * l + 2)
                ffn(2 * l + 1, 3 * l + 2)
                norm_pe(3 * l + 3)
            for m in range(DC):
                pe.wait_ge(fin_ready, m + 1)
                for tb in range(2):
                    nc.tensor.transpose(ps[2 * tb + m // 4][:, (m % 4) * P:(m % 4 + 1) * P],
                                        T[:, m % 2, tb * P:(tb + 1) * P], ident).then_inc(fin_T, 1)

        @block.scalar
        def _(act):
            av = nc.scalar.activation

            def hi(n0, j=0, i=0):
                s = (n0 + j) % RING
                if n0 + j >= PIECES and isinstance(i, int):
                    return
                if isinstance(i, int):
                    act.wait_ge(loaded[s], LOADED[n0 + j + 4 * i])
                    wait(act, w_used, n0 + j + 4 * i - RING + 1)
                else:
                    act.wait_ge(loaded[s], i * 16 + LOADED[n0 + j])
                    act.wait_ge(w_used, i * 4 + (n0 + j - RING + 1))
                av(wH[:, s, :], raw[:, s, :], ACT.Copy).then_inc(hi_done, 1)

            def norm_act(v, n0):
                t = T_NORM[v]
                for m in range(DC):
                    act.wait_ge(x_ready, x_count(v, m))
                    if m >= 2:
                        act.wait_ge(sq_used, DC * v + m - 1)
                    av(T[:, m % 2, 0:t], X[:, m, 0:t], ACT.Square).then_inc(sq_done, 1)
                act.wait_ge(sq_used, DC * (v + 1))
                nb = 2 * t // P
                av(root[:, 0, 0:nb], ps[4][:, 0:nb], ACT.Sqrt, bias=epsT[:, 0:1]).then_inc(rms, 1)
                if v == 6:
                    return
                shift = 9 * (v // 3) + 3 * (v % 3)
                for m in range(DC):
                    for hf in range(halves(t)):
                        c0 = h_count(v, m) - halves(t) + hf + 1
                        cs = slice(hf * SEQ, (hf + 1) * SEQ)
                        act.wait_ge(hp_done, c0)
                        av(hH[:, m, cs], T[:, m % 2, cs], ACT.Identity, bias=mod[:, shift, m, hf:hf + 1]).then_inc(h_hi, 1)
                    if m == 3:
                        hi(n0 + 2)
                    if m == 6:
                        hi(n0 + 3)

            def silu_evac(f, t, i):
                static = isinstance(i, int)
                for b in range(2):
                    act.wait_ge(w_used, i * RING + (FIRST["wi" + "12"[f % 2], f // 2] + 4))
                    wait(act, g_lo, i * 2 + 2 * GROUPS * f)
                    av(T[:, 2 + b, 0:t], ps[2 + b][:, 0:t], ACT.Silu).then_inc(g_silu, 1)
                for b in range(2):
                    act.wait_ge(g_prod, i * 2 + (2 * GROUPS * f + b + 1))
                    if static:
                        dst = GH[:, 2 * i + b, 0:t]
                    else:
                        dst = GH[:, bass.ds(i * 2 + b, 1), 0:t].rearrange("p a t -> p (a t)")
                    av(dst, T[:, 2 + b, 0:t], ACT.Copy).then_inc(g_hi, 1)

            def ffn_act(f, v):
                l, name = f // 2, "12"[f % 2]
                t = T_NORM[v]
                n0 = FIRST["wi" + name, l]

                n0w = n0

                def value_evac(i):
                    for b in range(2):
                        act.wait_ge(w_used, i * RING + (n0w + 2))
                        av(T[:, b, 0:t], ps[b][:, 0:t], ACT.Copy).then_inc(a_out, 1)

                def group(i):
                    hi(n0, 2, i)
                    hi(n0, 3, i)
                    silu_evac(f, t, i - 1)
                    hi(n0, 4, i)
                    hi(n0, 5, i)
                    value_evac(i)
                hi(n0, 4)
                hi(n0, 5)
                value_evac(0)
                group(1)
                with act.Fori(2, GROUPS - 1) as i:
                    group(i)
                i = GROUPS - 1
                hi(n0 + 4 * i + 2)
                hi(n0 + 4 * i + 3)
                silu_evac(f, t, i - 1)
                hi(n0 + 4 * i + 4)
                hi(n0 + 4 * i + 5)
                value_evac(i)
                silu_evac(f, t, i)
                n0 = FIRST["wo" + name, l]
                with act.Fori(0, FC // RING) as i:
                    for j in range(RING):
                        hi(n0, 2 + j, i)
                for j in range(FC // RING * RING, FC):
                    hi(n0 + 2 + j)

            def mixers_act(l):
                t = TOK if l == 0 else SEQ
                n0 = FIRST["proj", l]
                a0 = 26 * l
                def probs(s):
                    h = HEADS * l + STEP_HEAD[s]
                    for j in range(tiles(l)):
                        act.wait_ge(s_max, tile_count(l, s, j))
                        for q in range(2 if j == 2 else 1):
                            cs = slice(0, TOK) if j < 2 else slice(q * CTX, (q + 1) * CTX)
                            av(T[:, j, cs], ps[4 + j][:, cs], ACT.Exp, bias=stat[:, 1, j + q:j + q + 1], scale=SCALE,
                               accum_out=stat[:, 2, j + q:j + q + 1]).then_inc(p_exp, 1)
                    nq = 4 if l == 0 else 2
                    av(stat[:, 3, 0:nq], stat[:, 1, 0:nq], ACT.Exp, bias=sinkP[:, h:h + 1]).then_inc(p_exp, 1)

                def turned_probs(s):
                    for j in range(tiles(l)):
                        act.wait_ge(pt_mm, tile_count(l, s, j))
                        av(PTH[:, j, :], ps[4 + j][:], ACT.Copy).then_inc(pt_hi, 1)

                def head_out(s):
                    act.wait_ge(pv_mm, 8 * l + s + 1)
                    rows = slice((s % 2) * HD, (s % 2 + 1) * HD)
                    av(QH[rows, s // 2, 0:t], ps[7][rows, 0:t], ACT.Copy).then_inc(o_hi, 1)

                def unit_evac(u):
                    kind = UNITS[u]
                    act.wait_ge(w_used, n0 + 2 * u + 2)
                    banks = [ps[2 * (u % 2) + b] for b in range(2)]
                    if kind == "kv":
                        av(T[:, 3, :], banks[0][:], ACT.Copy).then_inc(proj_act, 1)
                        av(V32[:], banks[1][:], ACT.Copy).then_inc(proj_act, 1)
                    elif kind[0] == "q":
                        for b in range(2):
                            bi = 2 * int(kind[1]) + b
                            if bi == 3:
                                act.wait_ge(q_lo, 5 * l + 1)
                            av(T[:, bi, 0:t], banks[b][:, 0:t], ACT.Copy).then_inc(proj_act, 1)
                    elif kind[0] == "c":
                        if kind == "c1":
                            act.wait_ge(y_lo, 4 * l + 2)
                        for b in range(2):
                            av(cC[:, b, 0:t], banks[b][:, 0:t], ACT.Copy).then_inc(proj_act, 1)
                    else:
                        i = int(kind[1])
                        if i == 4:
                            act.wait_ge(y_lo, 4 * l + 4)
                        G = GA if i < 4 else GB
                        for b in range(2):
                            av(G[:, 2 * (i % 4) + b, 0:t], banks[b][:, 0:t], ACT.Tanh, scale=0.5
                               ).then_inc(proj_act, 1)

                def conv_high(pair):
                    for b in range(2):
                        act.wait_ge(proj_dve, 8 * l + 2 * DVE_UNITS.index(5 + 3 * pair) + b + 1)
                        av(YH[:, 2 * pair + b, 0:t], cY[:, b, 0:t], ACT.Copy).then_inc(y_hi, 1)

                for h in range(PROJ_P + 1):
                    if 2 <= h < PROJ_P:
                        hi(n0 + h + 2)
                    s, stage = divmod(h - HEAD0, 3)
                    if stage == 0 and 1 <= s <= HEADS:
                        head_out(s - 1)
                    if stage == 0 and 0 <= s < HEADS:
                        probs(s)
                    if stage == 2 and 0 <= s < HEADS:
                        turned_probs(s)
                    if h == 3:
                        act.wait_ge(rope_done, 5 * l + 1)
                        av(KH[:], T[:, 3, :], ACT.Copy).then_inc(q_hi, 1)
                        act.wait_ge(v_T, l + 1)
                        av(VH[:].rearrange("p b d -> p (b d)"), ps[6][:], ACT.Copy).then_inc(v_hi, 1)
                    if h in (5, 7):
                        for bi in (h - 5, h - 4):
                            act.wait_ge(rope_done, 5 * l + bi + 2)
                            av(QH[:, bi, 0:t], T[:, bi, 0:t], ACT.Copy).then_inc(q_hi, 1)
                    if h in (13, 19):
                        conv_high((h - 13) // 6)
                    if h % 2 == 0 and h >= 2 and h // 2 - 1 in ACT_UNITS:
                        unit_evac(h // 2 - 1)
                for n in range(FIRST["oa", l] + 2, FIRST["out", l] + 2):
                    hi(n)
                for m in range(DC):
                    act.wait_ge(ob_sum, 8 * l + m + 1)
                    av(hH[:, m, 0:t], GB[:, m, 0:t], ACT.Copy).then_inc(m_hi, 1)
                    if m in (0, 3):
                        hi(FIRST["out", l] + 2 + m // 3)
                for n in range(FIRST["out", l] + 4, FIRST["out", l] + DC + 2):
                    hi(n)

            hi(0)
            hi(1)
            act.wait_ge(vec_out, 1)
            act.wait_ge(vec_step, 1)
            av(cact[:].rearrange("p v k -> p (v k)"), VT[:, V_C:V_C + 16], ACT.Silu).then_inc(c_silu, 1)
            for l in range(DEPTH):
                norm_act(3 * l, FIRST["wi1", l])
                ffn_act(2 * l, 3 * l)
                norm_act(3 * l + 1, FIRST["proj", l])
                mixers_act(l)
                norm_act(3 * l + 2, FIRST["wi2", l])
                ffn_act(2 * l + 1, 3 * l + 2)
            norm_act(6, 0)

        @block.vector
        def _(dve):
            tt, ts, stt = nc.vector.tensor_tensor, nc.vector.tensor_scalar, nc.vector.scalar_tensor_tensor
            steps = [0]

            def mark(ins):
                steps[0] += 1
                ins.then_inc(vec_step, 1)

            def settle():
                dve.wait_ge(vec_step, steps[0])

            def lo(n0, j=0, i=0):
                s = (n0 + j) % RING
                if n0 + j >= PIECES and isinstance(i, int):
                    return
                dve.wait_ge(hi_done, n0 + j + 1 if isinstance(i, int) else i * 4 + (n0 + j + 1))
                tt(wL[:, s, :], raw[:, s, :], wH[:, s, :].bitcast(F32), ALU.subtract).then_inc(lo_done, 1)

            def rows_evac(base, i=None):
                dve.wait_ge(ada_used, 4 * (base + 1) if i is None else i * 4 + 4 * (base + 1))
                if i is not None or base > 0:
                    dve.wait_ge(ada_T, base if i is None else i + base)
                nc.vector.tensor_copy(rowS[:], ps[5][:]).then_inc(row_out, 1)

            def ada_evac(base, i=None):
                dve.wait_ge(ada_T, base + 1 if i is None else i + (base + 1))
                if i is None:
                    dst, bias = mod[:, base], VT[:, V_BADA + base * DC:V_BADA + (base + 1) * DC]
                else:
                    dst = mod[:, bass.ds(i + base, 1)].rearrange("p a k v -> p (a k) v")
                    bias = VT[:, bass.ds(i * DC + (V_BADA + base * DC), DC)]
                dst = dst.rearrange("p (h q) v -> p h q v", h=2)
                part = ps[6][:].rearrange("p (q e h r) -> p h q e r", q=4, e=2, h=2)
                bias = bias.rearrange("p (h q) -> p h q", h=2).unsqueeze(3).broadcast_to([P, 2, 4, 2])
                tt(dst, part[:, :, :, 0, 0:2], bias, ALU.add).then_inc(ada_part, 1)
                dve.wait_ge(ada_part, base + 1 if i is None else i + (base + 1))
                tt(dst, part[:, :, :, 1, 0:2], dst, ALU.add).then_inc(ada_out, 1)

            def norm_dve(v, n0):
                t = T_NORM[v]
                if v < 6:
                    mi = 9 * (v // 3) + 3 * (v % 3)
                    dve.wait_ge(ada_out, mi + 2)
                    mark(stt(normA[:, v], mod[:, mi + 1], 1.0,
                             VT[:, V_NORM + v * DC:V_NORM + (v + 1) * DC].unsqueeze(2).broadcast_to([P, DC, 2]),
                             ALU.add, ALU.mult))
                dve.wait_ge(rms, v + 1)
                nb = 2 * t // P
                mark(nc.vector.reciprocal(root[:, 1, 0:nb], root[:, 0, 0:nb]))
                settle()
                for tb in range(t // P):
                    ts(T[:, 2, tb * P:(tb + 1) * P], ident, root[:, 1, 2 * tb:2 * tb + 1], float(D),
                       ALU.mult, ALU.mult).then_inc(rms_diag, 1)
                dve.wait_ge(rms_row, v + 1)
                if v == 6:
                    for m in range(DC):
                        if m >= 2:
                            dve.wait_ge(fin_T, 2 * (m - 1))
                        stt(T[:, m % 2, 0:t], X[:, m, 0:t], VT[:, V_FIN + m:V_FIN + m + 1], ps[4][:, 0:t],
                            ALU.mult, ALU.mult).then_inc(fin_ready, 1)
                    return

                def scaled(m):
                    for hf in range(halves(t)):
                        cs = slice(hf * SEQ, (hf + 1) * SEQ)
                        stt(T[:, m % 2, cs], X[:, m, cs], normA[:, v, m, hf:hf + 1], ps[4][:, cs],
                            ALU.mult, ALU.mult).then_inc(hp_done, 1)

                def low(m):
                    for hf in range(halves(t)):
                        cs = slice(hf * SEQ, (hf + 1) * SEQ)
                        dve.wait_ge(h_hi, h_count(v, m) - halves(t) + hf + 1)
                        stt(hL[:, m, cs], T[:, m % 2, cs], mod[:, mi, m, hf:hf + 1], hH[:, m, cs].bitcast(F32),
                            ALU.add, ALU.subtract).then_inc(h_lo, 1)
                scaled(0)
                for m in range(DC):
                    if m + 1 < DC:
                        if m >= 1:
                            dve.wait_ge(h_lo, h_count(v, m - 1))
                        scaled(m + 1)
                    low(m)
                    if m == 3:
                        lo(n0 + 2)
                    if m == 6:
                        lo(n0 + 3)

            def residual(r):
                t = T_AFTER[r]
                l, q = (r - 1) // 3, (r - 1) % 3
                mi = 9 * l + 3 * q + 2
                dve.wait_ge(ada_out, mi + 1)
                mark(ts(gateH[:, r - 1], mod[:, mi], 0.5, None, ALU.mult))
                settle()
                for m in range(DC):
                    wait_chunk(dve, l, ("wo1", "out", "wo2")[q], m)
                    for hf in range(halves(t)):
                        cs = slice(hf * SEQ, (hf + 1) * SEQ)
                        stt(X[:, m, cs], ps[bank_of(m)][:, cs], gateH[:, r - 1, m, hf:hf + 1], X[:, m, cs],
                            ALU.mult, ALU.add).then_inc(x_ready, 1)

            def product(f, t, i):
                for b in range(2):
                    dve.wait_ge(g_silu, i * 2 + (2 * GROUPS * f + b + 1))
                    dve.wait_ge(a_out, i * 2 + (2 * GROUPS * f + b + 1))
                    tt(T[:, 2 + b, 0:t], T[:, 2 + b, 0:t], T[:, b, 0:t], ALU.mult).then_inc(g_prod, 1)
                for b in range(2):
                    dve.wait_ge(g_hi, i * 2 + (2 * GROUPS * f + b + 1))
                    if isinstance(i, int):
                        high, low = GH[:, 2 * i + b, 0:t], GL[:, 2 * i + b, 0:t]
                    else:
                        high = GH[:, bass.ds(i * 2 + b, 1), 0:t].rearrange("p a t -> p (a t)")
                        low = GL[:, bass.ds(i * 2 + b, 1), 0:t].rearrange("p a t -> p (a t)")
                    tt(low, T[:, 2 + b, 0:t], high.bitcast(F32), ALU.subtract).then_inc(g_lo, 1)

            def ffn_dve(f, v):
                l, name = f // 2, "12"[f % 2]
                t = T_NORM[v]
                n0 = FIRST["wi" + name, l]

                def group(i, ada0=None):
                    if ada0 is not None:
                        rows_evac(ada0 - 1, i)
                    lo(n0, 2, i)
                    lo(n0, 3, i)
                    product(f, t, i - 1)
                    if ada0 is not None:
                        ada_evac(ada0 - 1, i)
                    lo(n0, 4, i)
                    lo(n0, 5, i)
                lo(n0, 4)
                lo(n0, 5)
                ada0, count = ADA_IN_FFN.get(f, (None, 0))
                if count:
                    with dve.Fori(1, count + 1) as i:
                        group(i, ada0)
                if count + 1 < GROUPS - 1:
                    with dve.Fori(count + 1, GROUPS - 1) as i:
                        group(i)
                i = GROUPS - 1
                lo(n0 + 4 * i + 2)
                lo(n0 + 4 * i + 3)
                product(f, t, i - 1)
                lo(n0 + 4 * i + 4)
                lo(n0 + 4 * i + 5)
                product(f, t, i)
                n0 = FIRST["wo" + name, l]
                with dve.Fori(0, FC // RING) as i:
                    for j in range(RING):
                        lo(n0, 2 + j, i)
                for j in range(FC // RING * RING, FC):
                    lo(n0 + 2 + j)

            def rope_dve(l, bis):
                t = TOK if l == 0 else SEQ
                for bi in bis:
                    o = (bi + 1) % 5
                    dve.wait_ge(rope_mm, 5 * l + o + 1)
                    w = T[:, min(bi, 3), 0:SEQ]
                    mark(tt(ropeT[:, bi % 2, :], ps[4 + o % 2][:, 0:SEQ], sinT, ALU.mult))
                    mark(tt(w, w, cosT, ALU.mult))
                    settle()
                    tt(w, w, ropeT[:, bi % 2, :], ALU.add).then_inc(rope_done, 1)
                for bi in bis:
                    dve.wait_ge(q_hi, 5 * l + (bi + 1) % 5 + 1)
                    if bi < 4:
                        tt(QL[:, bi, 0:t], T[:, bi, 0:t], QH[:, bi, 0:t].bitcast(F32), ALU.subtract).then_inc(q_lo, 1)
                    else:
                        tt(KL[:], T[:, 3, :], KH[:].bitcast(F32), ALU.subtract).then_inc(q_lo, 1)

            def conv_taps(l, pair):
                segs = 2 if l == 0 else 1
                for k in range(CONV_K):
                    for b in range(2):
                        tap = VT[:, V_CONV + (l * CONV_K + k) * CC + 2 * pair + b:][:, 0:1]
                        src = cU[:, b, 0:segs, k:k + SEQ]
                        dst = cY[:, b, 0:segs * SEQ].rearrange("p (s t) -> p s t", s=segs)
                        if k == 0:
                            mark(ts(dst, src, tap, None, ALU.mult))
                        else:
                            mark(stt(dst, src, tap, dst, ALU.mult, ALU.add))
                    settle()

            def y_low(l, pair, t):
                for b in range(2):
                    dve.wait_ge(y_hi, 4 * l + 2 * pair + b + 1)
                    tt(YL[:, 2 * pair + b, 0:t], cY[:, b, 0:t], YH[:, 2 * pair + b, 0:t].bitcast(F32),
                       ALU.subtract).then_inc(y_lo, 1)

            def mixers_dve(l):
                t = TOK if l == 0 else SEQ
                segs = t // SEQ
                n0 = FIRST["proj", l]
                mark(nc.vector.memset(cU[:].rearrange("p a b c -> p (a b c)"), 0.0))
                settle()
                def unit_evac(u):
                    kind = UNITS[u]
                    dve.wait_ge(w_used, n0 + 2 * u + 2)
                    banks = [ps[2 * (u % 2) + b] for b in range(2)]
                    if kind[0] == "u":
                        dve.wait_ge(proj_act, 26 * l + 2 * ACT_UNITS.index(u - 1) + 2)
                        for b in range(2):
                            tt(cU[:, b, 0:segs, 1:SEQ + 1], banks[b][:, 0:t].rearrange("p (s t) -> p s t", s=segs),
                               cC[:, b, 0:t].rearrange("p (s t) -> p s t", s=segs), ALU.mult).then_inc(proj_dve, 1)
                        dve.wait_ge(proj_dve, 8 * l + 2 * DVE_UNITS.index(u) + 2)
                        conv_taps(l, int(kind[1]))
                    else:
                        for b in range(2):
                            w = cY[:, b, 0:t]
                            tt(w, banks[b][:, 0:t], w, ALU.mult).then_inc(proj_dve, 1)

                def maxima(s):
                    h = HEADS * l + STEP_HEAD[s]
                    for j, (edge, cs) in enumerate(((mask0, slice(P, 2 * P)), (mask1, slice(0, P)))):
                        dve.wait_ge(s_mm, tile_count(l, s, j))
                        mark(tt(ps[4 + j][:, cs], ps[4 + j][:, cs], edge, ALU.add))
                    for j in range(tiles(l)):
                        if j == 2:
                            dve.wait_ge(s_mm, tile_count(l, s, 2))
                            nq, src = 2, ps[6][:].rearrange("p (q k) -> p q k", q=2)
                        else:
                            if j == 0:
                                settle()
                            nq, src = 1, ps[4 + j][:]
                        mark(nc.vector.tensor_reduce(stat[:, 0, j:j + nq], src, AX_X, ALU.max))
                        settle()
                        ts(stat[:, 1, j:j + nq], stat[:, 0, j:j + nq], -SCALE, sinkN[:, h:h + 1], ALU.mult, ALU.min
                           ).then_inc(s_max, 1)

                def normalise(s):
                    nq = 4 if l == 0 else 2
                    dve.wait_ge(p_exp, (nq + 1) * (s + 1) + (40 if l else 0))
                    mark(tt(stat[:, 4, 0:nq], stat[:, 2, 0:nq], stat[:, 3, 0:nq], ALU.add))
                    settle()
                    mark(nc.vector.reciprocal(stat[:, 5, 0:nq], stat[:, 4, 0:nq]))
                    settle()
                    for j in range(tiles(l)):
                        for q in range(2 if j == 2 else 1):
                            cs = slice(0, TOK) if j < 2 else slice(q * CTX, (q + 1) * CTX)
                            ins = ts(T[:, j, cs], T[:, j, cs], stat[:, 5, j + q:j + q + 1], None, ALU.mult)
                            if j == 2 and q == 0:
                                mark(ins)
                                settle()
                            else:
                                ins.then_inc(p_norm, 1)

                def turned_probs(s):
                    for j in range(tiles(l)):
                        dve.wait_ge(pt_hi, tile_count(l, s, j))
                        tt(PTL[:, j, :], ps[4 + j][:], PTH[:, j, :].bitcast(F32), ALU.subtract).then_inc(pt_lo, 1)

                def head_out(s):
                    dve.wait_ge(o_hi, 8 * l + s + 1)
                    rows = slice((s % 2) * HD, (s % 2 + 1) * HD)
                    tt(QL[rows, s // 2, 0:t], ps[7][rows, 0:t], QH[rows, s // 2, 0:t].bitcast(F32),
                       ALU.subtract).then_inc(o_lo, 1)

                for h in range(PROJ_P):
                    if h >= 2:
                        lo(n0 + h + 2)
                    s, stage = divmod(h - HEAD0, 3)
                    if stage == 0 and 1 <= s <= HEADS:
                        head_out(s - 1)
                    if stage == 0 and 0 <= s < HEADS:
                        maxima(s)
                    if stage == 1 and 0 <= s < HEADS:
                        normalise(s)
                    if stage == 2 and 0 <= s < HEADS:
                        turned_probs(s)
                    if h == 3:
                        rope_dve(l, (4,))
                        dve.wait_ge(v_hi, l + 1)
                        tt(VL[:].rearrange("p b d -> p (b d)"), ps[6][:],
                           VH[:].rearrange("p b d -> p (b d)").bitcast(F32), ALU.subtract).then_inc(v_lo, 1)
                    if h in (5, 7):
                        rope_dve(l, (h - 5, h - 4))
                    if h in (13, 19):
                        y_low(l, (h - 13) // 6, t)
                    if h % 2 == 0 and h >= 2 and h // 2 - 1 in DVE_UNITS:
                        unit_evac(h // 2 - 1)
                for n in range(FIRST["oa", l] + 2, FIRST["oa", l] + 6):
                    lo(n)
                for m in range(DC):
                    wait_chunk(dve, l, "oa", m)
                    stt(GA[:, m, 0:t], GA[:, m, 0:t], 1.0, ps[bank_of(m)][:, 0:t], ALU.add, ALU.mult
                        ).then_inc(oa_out, 1)
                for n in range(FIRST["ob", l] + 2, FIRST["ob", l] + 6):
                    lo(n)
                dve.wait_ge(oa_out, 8 * (l + 1))

                def branch_gate(m):
                    wait_chunk(dve, l, "ob", m)
                    stt(GB[:, m, 0:t], GB[:, m, 0:t], 1.0, ps[bank_of(m)][:, 0:t], ALU.add, ALU.mult
                        ).then_inc(ob_out, 1)

                def branch_sum(m):
                    dve.wait_ge(ob_out, 8 * l + m + 1)
                    tt(GB[:, m, 0:t], GB[:, m, 0:t], GA[:, m, 0:t], ALU.add).then_inc(ob_sum, 1)

                def branch_low(m):
                    dve.wait_ge(m_hi, 8 * l + m + 1)
                    tt(hL[:, m, 0:t], GB[:, m, 0:t], hH[:, m, 0:t].bitcast(F32), ALU.subtract).then_inc(m_lo, 1)
                branch_gate(0)
                branch_gate(1)
                branch_sum(0)
                branch_gate(2)
                branch_low(0)
                for m in range(3, DC):
                    branch_gate(m)
                lo(FIRST["out", l] + 2)
                branch_sum(1)
                for m in range(1, DC):
                    if m + 1 < DC:
                        branch_sum(m + 1)
                    branch_low(m)
                    if m == 3:
                        lo(FIRST["out", l] + 3)
                for n in range(FIRST["out", l] + 4, FIRST["out", l] + DC + 2):
                    lo(n)

            nc.vector.memset(ps[5][:], 0.0).then_inc(bank5_zero, 1)
            lo(0)
            lo(1)
            dve.wait_ge(vec_T, 1)
            nc.vector.tensor_copy(VT[:], ps[6][:, 0:NVEC]).then_inc(vec_out, 1)
            mark(nc.vector.memset(epsT[:], EPS))
            dve.wait_ge(in_sink, 16)
            mark(ts(sinkN[:], sinkP[:], -1.0, None, ALU.mult))
            for m in range(DC):
                dve.wait_ge(x_T, m + 1)
                nc.vector.tensor_copy(X[:, m, :], ps[m % 4][:]).then_inc(x_ready, 1)
            dve.wait_ge(vec_out, 1)
            for j in range(2):
                rows_evac(j)
                ada_evac(j)
            for l in range(DEPTH):
                norm_dve(3 * l, FIRST["wi1", l])
                ffn_dve(2 * l, 3 * l)
                residual(3 * l + 1)
                norm_dve(3 * l + 1, FIRST["proj", l])
                mixers_dve(l)
                residual(3 * l + 2)
                if l == 0:
                    dve.wait_ge(x_ready, x_count(2, DC - 1))
                    nc.vector.memset(ps[5][:], 0.0).then_inc(bank5_zero, 1)
                norm_dve(3 * l + 2, FIRST["wi2", l])
                ffn_dve(2 * l + 1, 3 * l + 2)
                residual(3 * l + 3)
            norm_dve(6, 0)
            for tb in range(2):
                for half in range(2):
                    dve.wait_ge(fin_T, 2 * DC if half else DC - 1 + tb)
                    nc.vector.tensor_copy(yout[:, tb, half * TOK:(half + 1) * TOK], ps[2 * tb + half][:]
                                          ).then_inc(fin_out, 1)


_INS = ["x", "c", "ctx", "c_ctx", "w_ada", "b_ada", "norm_w", "ffn1_wi", "ffn1_wo", "w_in", "conv_w", "sink", "w_oa",
        "w_ob", "w_out", "ffn2_wi", "ffn2_wo", "final_norm_w"]


def kernel(**inputs):
    import concourse.bacc as bacc
    from concourse.bass_utils import run_bass_kernel_spmd

    nc = bacc.Bacc("TRN2", target_bir_lowering=False, num_devices=1)
    arrays, args = {}, []
    for name in _INS + ["shape_consts"]:
        a = shape_constants() if name == "shape_consts" else np.ascontiguousarray(inputs[name])
        arrays[f"in_{name}"] = a
        args.append(nc.dram_tensor(f"in_{name}", a.shape, mybir.dt.from_np(a.dtype), kind="ExternalInput").ap())
    args.append(nc.dram_tensor("out", (1, SEQ, D), F32, kind="ExternalOutput").ap())
    build(nc, *args)
    r = run_bass_kernel_spmd(nc, [arrays], core_ids=[0])
    return r.results[0]["out"]
```

```python
from contextlib import ExitStack

import numpy as np

import concourse.bass as bass
from concourse import mybir

P = 128
F32 = mybir.dt.float32
F32R = mybir.dt.float32r
ALU = mybir.AluOpType
ACT = mybir.ActivationFunctionType
AX_X = mybir.AxisListType.X

D = 1024
DC = D // P
SEQ = 256
CTX = 256
TOK = SEQ + CTX
DEPTH = 2
NMOD = 9
HEADS, KV_HEADS, HD = 8, 2, 64
ATTN_W, KV_W, CONV_W = HEADS * HD, KV_HEADS * HD, D // 2
CC = CONV_W // P
CONV_K = 3
WINDOW = 128
GRID_W = 64
DFF = 2816
FC = DFF // P
GROUPS = FC // 2
EPS = 1e-6
SCALE = HD ** -0.5
NEG = -1e30

Q0 = 0
K0 = ATTN_W
B0 = ATTN_W + 2 * KV_W
C0 = B0 + CONV_W
U0 = C0 + CONV_W
GA0 = U0 + CONV_W
GB0 = GA0 + D

RING = 4
PIECE = 8 * P

V_NORM, V_CONV, V_FIN, V_C = 0, 48, 72, 80
V_BADA = 96
NVEC = V_BADA + DEPTH * NMOD * DC


def shape_constants():
    d = np.arange(P) % HD
    t = np.arange(SEQ)
    pos = np.where((d < HD // 2)[:, None], (t // GRID_W)[None, :], (t % GRID_W)[None, :]).astype(np.float32)
    inv = (np.float32(10000.0) ** (-(d % (HD // 4)).astype(np.float32) / np.float32(HD // 4))).astype(np.float32)
    ang = (pos * inv[:, None]).astype(np.float32)
    rot = np.zeros((P, P))
    for i in range(P):
        if i % (HD // 2) < HD // 4:
            rot[i + HD // 4, i] = -1.0
        else:
            rot[i - HD // 4, i] = 1.0
    q, k = np.arange(P)[:, None], np.arange(P)[None, :]
    return np.concatenate([np.cos(ang), np.sin(ang), rot, np.eye(P), np.full((P, P), 1.0 / D),
                           np.where(k <= q, 0.0, NEG), np.where(k >= q, 0.0, NEG)], axis=1).astype(np.float32)


N_CONST = 2 * SEQ + 5 * P

WI_P, WO_P, OA_P, OB_P, OUT_P = 4 * GROUPS, FC, CC, CC, DC
UNITS = ["kv", "q0", "q1", "c0", "u0", "b0", "c1", "u1", "b1"] + [f"g{i}" for i in range(8)]
PROJ_P = 2 * len(UNITS)
ACT_UNITS = [u for u, k in enumerate(UNITS) if k[0] in "qkcg"]
DVE_UNITS = [u for u, k in enumerate(UNITS) if k[0] in "ub"]


def piece_plan():
    first, n, ways = {}, 0, []
    for l in range(DEPTH):
        for name, count in (("wi1", WI_P), ("wo1", WO_P), ("proj", PROJ_P), ("oa", OA_P), ("ob", OB_P),
                            ("out", OUT_P), ("wi2", WI_P), ("wo2", WO_P)):
            first[name, l] = n
            ways += [4 if name == "proj" and 2 <= j < 6 else 2 if name == "oa" else 1 for j in range(count)]
            n += count
    at, loaded = [0] * RING, []
    for j, w in enumerate(ways):
        at[j % RING] += 16 * w
        loaded.append(at[j % RING])
    return first, loaded, n


FIRST, LOADED, PIECES = piece_plan()
ADA_IN_FFN = {0: (2, 7, 1), 1: (9, 9, 0)}
HEAD0 = 8
STEP_HEAD = [b + 4 * r for b in range(4) for r in range(2)]


def bank_of(m):
    return (m + 4) % 8


def build(nc, x, c, ctx, c_ctx, w_ada, b_ada, norm_w, ffn1_wi, ffn1_wo, w_in, conv_w, sink, w_oa, w_ob, w_out,
          ffn2_wi, ffn2_wo, final_norm_w, consts, out):
    stack = ExitStack()
    with stack:
        def sb(name, shape, dt=F32):
            return stack.enter_context(nc.sbuf_tensor(name, shape, dt))

        def sem(name):
            return stack.enter_context(nc.semaphore(name))

        X = sb("X", [P, DC, TOK])
        hH = sb("hH", [P, DC, TOK], F32R)
        hL = sb("hL", [P, DC, TOK], F32R)
        raw = sb("raw", [P, RING, PIECE])
        wH = sb("wH", [P, RING, PIECE], F32R)
        wL = sb("wL", [P, RING, PIECE], F32R)
        T = sb("T", [P, 4, TOK])
        cst = sb("cst", [P, N_CONST])
        VT = sb("VT", [P, NVEC])
        mod = sb("mod", [P, DEPTH * NMOD, DC, 2])
        normA = sb("normA", [P, 3 * DEPTH, DC, 2])
        gateH = sb("gateH", [P, 3 * DEPTH, DC, 2])
        cact = sb("cact", [P, 2, DC])
        sinkP = sb("sinkP", [P, DEPTH * HEADS])
        sinkN = sb("sinkN", [P, DEPTH * HEADS])
        epsT = sb("epsT", [P, 1])
        root = sb("root", [P, 2, 8])
        stat = sb("stat", [P, 6, 4])
        with ExitStack() as r:
            adaA = r.enter_context(nc.sbuf_tensor("adaA", [P, 2, D], F32))
            with ExitStack() as s:
                GH = s.enter_context(nc.sbuf_tensor("GH", [P, FC, TOK], F32R))
                GL = s.enter_context(nc.sbuf_tensor("GL", [P, FC, TOK], F32R))
            with ExitStack() as s:
                s.enter_context(nc.sbuf_tensor("hidden_front", [P, FC - 4, TOK], F32))
                rowS = s.enter_context(nc.sbuf_tensor("rowS", [P, TOK], F32))
                s.enter_context(nc.sbuf_tensor("hidden_mid", [P, 3 + FC - 4, TOK], F32))
                adaB = s.enter_context(nc.sbuf_tensor("adaB", [P, 2, D], F32))
            with ExitStack() as s:
                s.enter_context(nc.sbuf_tensor("before_squares", [P, 36, TOK], F32))
                sqT = s.enter_context(nc.sbuf_tensor("sqT", [P, 4, TOK], F32))
            with ExitStack() as s:
                def mb(name, shape, dt=F32):
                    return s.enter_context(nc.sbuf_tensor(name, shape, dt))
                QH = mb("QH", [P, 4, TOK], F32R)
                QL = mb("QL", [P, 4, TOK], F32R)
                KH = mb("KH", [P, TOK], F32R)
                KL = mb("KL", [P, TOK], F32R)
                V32 = mb("V32", [P, TOK])
                VH = mb("VH", [P, 4, P], F32R)
                VL = mb("VL", [P, 4, P], F32R)
                YH = mb("YH", [P, CC, TOK], F32R)
                YL = mb("YL", [P, CC, TOK], F32R)
                GA = mb("GA", [P, DC, TOK])
                PTH = mb("PTH", [P, 3, TOK], F32R)
                PTL = mb("PTL", [P, 3, TOK], F32R)
                with ExitStack() as s2:
                    GB = s2.enter_context(nc.sbuf_tensor("GB", [P, DC, TOK], F32))
                cC = mb("cC", [P, 2, TOK])
                cU = mb("cU", [P, 2, 2, SEQ + 2])
                cY = mb("cY", [P, 2, TOK])
                ropeT = mb("ropeT", [P, 2, SEQ])
            with ExitStack() as s:
                xin = s.enter_context(nc.sbuf_tensor("xin", [P, 4, D], F32))
                vin = s.enter_context(nc.sbuf_tensor("vin", [P, 3, P], F32))
                ada0a = s.enter_context(nc.sbuf_tensor("ada0a", [P, 4, D], F32))
                s.enter_context(nc.sbuf_tensor("around_rows", [P, 9, P], F32))
                ada0b = s.enter_context(nc.sbuf_tensor("ada0b", [P, 8, D], F32))
            with ExitStack() as s:
                yout = s.enter_context(nc.sbuf_tensor("yout", [P, 2, D], F32))
        ps = [stack.enter_context(nc.psum_tensor(f"ps{i}", [P, TOK], F32)) for i in range(8)]

        cosT, sinT = cst[:, 0:SEQ], cst[:, SEQ:2 * SEQ]
        o = 2 * SEQ
        ada0 = [ada0a[:, k] for k in range(4)] + [ada0b[:, k] for k in range(8)] + [xin[:, k] for k in range(4)]
        ada = [adaA[:, 0], adaA[:, 1], adaB[:, 0], adaB[:, 1]]
        rotM, ident, meanM, mask0, mask1 = (cst[:, o + j * P:o + (j + 1) * P] for j in range(5))

        loaded = [sem(f"loaded{i}") for i in range(RING)]
        hi_done = sem("hi_done")
        lo_done = sem("lo_done")
        w_used = sem("w_used")
        in_vec, in_x, in_c, in_sink = sem("in_vec"), sem("in_x"), sem("in_c"), sem("in_sink")
        ada0_loaded = [sem(f"ada0_loaded{i}") for i in range(4)]
        ada_loaded = [sem(f"ada_loaded{i}") for i in range(4)]
        ada_used = sem("ada_used")
        bank5_zero = sem("bank5_zero")
        row_out = sem("row_out")
        ada_T = sem("ada_T")
        ada_part = sem("ada_part")
        ada_out = sem("ada_out")
        vec_T, vec_out, c_silu = sem("vec_T"), sem("vec_out"), sem("c_silu")
        x_T = sem("x_T")
        x_ready = sem("x_ready")
        sq_done = sem("sq_done")
        sq_four = sem("sq_four")
        sq_pair = sem("sq_pair")
        mean_mm = sem("mean_mm")
        rms = sem("rms")
        rms_diag = sem("rms_diag")
        rms_row = sem("rms_row")
        hp_done = sem("hp_done")
        h_hi, h_lo = sem("h_hi"), sem("h_lo")
        a_out, g_silu = sem("a_out"), sem("g_silu")
        g_prod, g_hi, g_lo = sem("g_prod"), sem("g_hi"), sem("g_lo")
        acc_mm = sem("acc_mm")
        oa_out, ob_out, ob_sum = sem("oa_out"), sem("ob_out"), sem("ob_sum")
        m_hi, m_lo = sem("m_hi"), sem("m_lo")
        proj_act, proj_dve = sem("proj_act"), sem("proj_dve")
        rope_mm, rope_done, q_hi, q_lo = sem("rope_mm"), sem("rope_done"), sem("q_hi"), sem("q_lo")
        v_T, v_hi, v_lo = sem("v_T"), sem("v_hi"), sem("v_lo")
        y_hi, y_lo = sem("y_hi"), sem("y_lo")
        s_mm, s_max, p_exp, p_norm = sem("s_mm"), sem("s_max"), sem("p_exp"), sem("p_norm")
        pt_mm, pt_hi, pt_lo = sem("pt_mm"), sem("pt_hi"), sem("pt_lo")
        pv_mm, o_hi, o_lo = sem("pv_mm"), sem("o_hi"), sem("o_lo")
        vec_step = sem("vec_step")
        fin_ready, fin_T, fin_out, stored = sem("fin_ready"), sem("fin_T"), sem("fin_out"), sem("stored")

        def wait(eng, s, v):
            if not isinstance(v, int) or v > 0:
                eng.wait_ge(s, v)

        T_AFTER = [TOK, TOK, TOK, TOK, TOK, SEQ, SEQ]
        T_NORM = [TOK, TOK, TOK, TOK, TOK, SEQ, SEQ]

        def halves(t):
            return t // SEQ

        def x_count(r, m):
            n = sum(DC * (1 if q == 0 else halves(T_AFTER[q])) for q in range(r))
            return n + (m + 1) * (1 if r == 0 else halves(T_AFTER[r]))

        def h_count(v, m):
            return sum(DC * halves(T_NORM[q]) for q in range(v)) + (m + 1) * halves(T_NORM[v])

        def tiles(l):
            return 3 if l == 0 else 2

        def tile_count(l, s, j):
            return (0 if l == 0 else 8 * 3) + s * tiles(l) + j + 1

        def wait_chunk(eng, l, name, m):
            idx = ("wo1", "oa", "ob", "out", "wo2").index(name)
            if m < DC - 1:
                eng.wait_ge(acc_mm, (DC - 1) * (5 * l + idx) + m + 1)
            else:
                pieces = {"wo1": WO_P, "oa": OA_P, "ob": OB_P, "out": OUT_P, "wo2": WO_P}[name]
                eng.wait_ge(w_used, FIRST[name, l] + pieces)

        squares = [T[:, m] for m in range(4)] + [sqT[:, m] for m in range(4)]
        SUM_TILES = (0, 4, 6)
        BUSY = (5, 6, 8)

        block = stack.enter_context(nc.Block())

        @block.sync
        def _(sp):
            sp.dma_start(vin[0:48, 0, :], norm_w.rearrange("l j (k p) -> (l j k) p", p=P)).then_inc(in_vec, 16)
            sp.dma_start(vin[V_CONV:72, 0, :], conv_w.rearrange("l j (k p) -> (l j k) p", p=P)).then_inc(in_vec, 16)
            sp.dma_start(vin[V_FIN:80, 0, :], final_norm_w.rearrange("(k p) -> k p", p=P)).then_inc(in_vec, 16)
            sp.dma_start(vin[V_C:88, 0, :], c.rearrange("b (k p) -> (b k) p", p=P)).then_inc(in_vec, 16)
            sp.dma_start(vin[88:96, 0, :], c_ctx.rearrange("(k p) -> k p", p=P)).then_inc(in_vec, 16)
            for l in range(DEPTH):
                sp.dma_start(vin[0:NMOD * DC, 1 + l, :],
                             b_ada[l].rearrange("(k p) -> k p", p=P)).then_inc(in_vec, 16)
            sp.dma_start(sinkP[:], sink.rearrange("l h -> (l h)").partition_broadcast(P)).then_inc(in_sink, 16)
            sp.dma_start(cst[:], consts).then_inc(in_c, 16)
            sp.dma_start(xin[:, 0:2, :], x[0].rearrange("(t p) d -> p t d", p=P)).then_inc(in_x, 16)
            sp.dma_start(xin[:, 2:4, :], ctx[0].rearrange("(t p) d -> p t d", p=P)).then_inc(in_x, 16)

            def first_ada(h):
                for kk, dst in enumerate((ada0a[:], ada0b[:, 0:4]) if h == 0 else (ada0b[:, 4:8], xin[:])):
                    for j in range(2):
                        sp.dma_start(dst[:, :, j * TOK:(j + 1) * TOK],
                                     w_ada[0].rearrange("(k p) n -> p k n", p=P)[:, 4 * kk:4 * kk + 4,
                                                                                 j * D + h * TOK:j * D + (h + 1) * TOK]
                                     ).then_inc(ada0_loaded[2 * h + kk], 16)
            first_ada(0)

            def slot_free(n0, j, i=0):
                if isinstance(i, int):
                    wait(sp, lo_done, n0 + j + 4 * i - RING + 1)
                else:
                    sp.wait_ge(lo_done, i * 4 + (n0 + j - RING + 1))

            def load_columns(n0, j, src, kh, col, i=0):
                slot_free(n0, j, i)
                s = (n0 + j) % RING
                sp.dma_start(raw[:, s, :].rearrange("p (k n) -> p k n", k=4),
                             src.rearrange("(k p) n -> p k n", p=P)[:, 4 * kh:4 * kh + 4, bass.ds(col, 2 * P)]
                             ).then_inc(loaded[s], 16)

            def load_rows(n0, j, src, k, i=0):
                slot_free(n0, j, i)
                s = (n0 + j) % RING
                sp.dma_start(raw[:, s, :], src[bass.ds(k * P, P), :]).then_inc(loaded[s], 16)

            def ffn_loads(l, name, wi, wo):
                n0 = FIRST["wi" + name, l]

                def group(i, half):
                    for j in range(2 * half, 2 * half + 2):
                        load_columns(n0, j, wi, half, i * (2 * P) + (j % 2) * DFF, i)
                group(0, 0)
                if n0 == 0:
                    sp.wait_ge(x_T, DC)
                    first_ada(1)
                group(0, 1)
                with sp.Fori(1, GROUPS) as i:
                    group(i, 0)
                    group(i, 1)
                n0 = FIRST["wo" + name, l]
                with sp.Fori(0, FC // RING) as i:
                    for j in range(RING):
                        load_rows(n0, j, wo, i * RING + j, i)
                for j in range(FC // RING * RING, FC):
                    load_rows(n0, j, wo, j)

            for l in range(DEPTH):
                ffn_loads(l, "1", ffn1_wi[l], ffn1_wo[l])
                n0 = FIRST["proj", l]
                wv = w_in[l].rearrange("(k p) n -> p k n", p=P)
                for u, kind in enumerate(UNITS[:9]):
                    i = int(kind[1]) if kind != "kv" else 0
                    for kh in range(2):
                        if kind[0] == "q":
                            n = n0 + 2 * u + kh
                            slot_free(n, 0)
                            dst = raw[:, n % RING, :].rearrange("p (k b r d) -> p k b r d", k=4, b=2, r=2)
                            for b in range(2):
                                for r in range(2):
                                    col = Q0 + (2 * i + b + 4 * r) * HD
                                    sp.dma_start(dst[:, :, b, r, :], wv[:, 4 * kh:4 * kh + 4, col:col + HD]
                                                 ).then_inc(loaded[n % RING], 16)
                        else:
                            col = {"k": K0, "b": B0, "c": C0, "u": U0}[kind[0]] + 2 * P * i
                            load_columns(n0 + 2 * u + kh, 0, w_in[l], kh, col)
                with sp.Fori(0, 4) as i:
                    for j in range(4):
                        load_columns(n0 + 18, j, w_in[l], j % 2, i * (4 * P) + (j // 2) * 2 * P + GA0, i)
                for b in range(4):
                    n = FIRST["oa", l] + b
                    slot_free(n, 0)
                    for r in range(2):
                        sp.dma_start(raw[r * HD:(r + 1) * HD, n % RING, :],
                                     w_oa[l, (b + 4 * r) * HD:(b + 4 * r + 1) * HD, :]).then_inc(loaded[n % RING], 16)
                for k in range(4):
                    load_rows(FIRST["ob", l], k, w_ob[l], k)
                for k in range(DC):
                    load_rows(FIRST["out", l], k, w_out[l], k)
                ffn_loads(l, "2", ffn2_wi[l], ffn2_wo[l])
            for tb in range(2):
                sp.wait_ge(fin_out, 2 * tb + 2)
                sp.dma_start(out[0, tb * P:(tb + 1) * P, :], yout[:, tb, :]).then_inc(stored, 16)
            sp.wait_ge(stored, 32)

        @block.gpsimd
        def _(pool):
            def load_ada(mi, k, base, i=None):
                l, j = mi
                need = 4 * base + k // 2 - 1
                if i is None:
                    wait(pool, ada_used, need)
                    src = w_ada[l, k * P:(k + 1) * P, j * D:(j + 1) * D]
                else:
                    pool.wait_ge(ada_used, i * 4 + need)
                    src = w_ada[l, k * P:(k + 1) * P, bass.ds(i * D + j * D, D)]
                pool.dma_start(ada[k % 4], src).then_inc(ada_loaded[k % 4], 16)

            def add_squares(v):
                t = T_NORM[v]
                for i, (m, k) in enumerate(((0, 1), (2, 3), (0, 2))):
                    if i < 2:
                        pool.wait_ge(sq_done, DC * v + k + 1)
                    else:
                        pool.wait_ge(sq_four, 3 * v + 2)
                    nc.gpsimd.tensor_tensor(squares[m][:, 0:t], squares[m][:, 0:t], squares[k][:, 0:t], ALU.add
                                            ).then_inc(sq_four, 1)

            add_squares(0)
            pool.wait_ge(ada_used, 8)
            for k in range(4):
                pool.dma_start(ada[k], w_ada[0, k * P:(k + 1) * P, 2 * D:3 * D]).then_inc(ada_loaded[k], 16)
            for k in range(4, DC):
                load_ada((0, 2), k, 2)
            with pool.Fori(1, 7) as i:
                for k in range(DC):
                    load_ada((0, 2), k, 2, i)
            add_squares(1)
            add_squares(2)
            with pool.Fori(0, NMOD) as i:
                for k in range(DC):
                    load_ada((1, 0), k, 9, i)
            for v in range(3, 7):
                add_squares(v)

        @block.tensor
        def _(pe):
            mm = nc.tensor.matmul

            def triple(dst, wa, wb, ra, rb, start, stop, group_check=True):
                kw = {} if group_check else {"skip_group_check": True}
                mm(dst, wa, ra, start=start, stop=False, **kw)
                mm(dst, wa, rb, start=False, stop=False, **kw)
                return mm(dst, wb, ra, start=False, stop=stop, **kw)

            def ada_pair(p, base, i=None):
                first = i is None and base < 2
                for k in (2 * p, 2 * p + 1):
                    if first:
                        pe.wait_ge(ada0_loaded[2 * base + k // 4], 32)
                        continue
                    count = 16 * (2 * (base - 2) + k // 4 + 1)
                    pe.wait_ge(ada_loaded[k % 4], count if i is None else i * 32 + count)
                if p == 0:
                    if i is None:
                        wait(pe, row_out, base)
                    else:
                        pe.wait_ge(row_out, i + base)
                for k in (2 * p, 2 * p + 1):
                    src = ada0[8 * base + k] if first else ada[k % 4]
                    for h in range(2):
                        g = 2 * (k % 2) + h
                        last = mm(ps[5][32 * g:32 * g + 2, :], cact[:, :, k], src[:, h * TOK:(h + 1) * TOK],
                                  start=(p == 0), stop=(p == 3), skip_group_check=True)
                last.then_inc(ada_used, 1)

            def ada_turn(base, i=None):
                pe.wait_ge(row_out, base + 1 if i is None else i + (base + 1))
                if i is None:
                    wait(pe, ada_out, base)
                else:
                    pe.wait_ge(ada_out, i + base)
                for q in range(4):
                    last = nc.tensor.transpose(ps[6][:, q * P:(q + 1) * P], rowS[:, q * P:(q + 1) * P], ident)
                last.then_inc(ada_T, 1)

            def columns_piece(n0, j, banks, kh, t, i=0, v=None, midway=None):
                s = (n0 + j) % RING
                pe.wait_ge(lo_done, i * 4 + (n0 + j + 1))
                for k in range(4):
                    if k == 2 and midway is not None:
                        midway()
                    kk = 4 * kh + k
                    ws = [slice(k * 2 * P + b * P, k * 2 * P + (b + 1) * P) for b in range(2)]
                    if v is not None:
                        pe.wait_ge(h_hi, h_count(v, kk))
                        for b, w in enumerate(ws):
                            mm(ps[banks + b][:, 0:t], wH[:, s, w], hH[:, kk, 0:t], start=(kk == 0), stop=False,
                               skip_group_check=True)
                            mm(ps[banks + b][:, 0:t], wL[:, s, w], hH[:, kk, 0:t], start=False, stop=False,
                               skip_group_check=True)
                        pe.wait_ge(h_lo, h_count(v, kk))
                        for b, w in enumerate(ws):
                            last = mm(ps[banks + b][:, 0:t], wH[:, s, w], hL[:, kk, 0:t], start=False,
                                      stop=(kk == DC - 1), skip_group_check=True)
                        continue
                    for b, w in enumerate(ws):
                        last = triple(ps[banks + b][:, 0:t], wH[:, s, w], wL[:, s, w], hH[:, kk, 0:t], hL[:, kk, 0:t],
                                      kk == 0, kk == DC - 1, False)
                last.then_inc(w_used, 1)

            def rows_piece(n0, j, k, ra, rb, t, start, stop, i=0, bank_wait=None):
                s = (n0 + j) % RING
                pe.wait_ge(lo_done, i * 4 + (n0 + j + 1))
                for m in range(DC):
                    if bank_wait is not None:
                        bank_wait(m)
                    last = triple(ps[bank_of(m)][:, 0:t], wH[:, s, m * P:(m + 1) * P], wL[:, s, m * P:(m + 1) * P],
                                  ra[:, bass.ds(k, 1), 0:t].rearrange("p a t -> p (a t)") if not isinstance(k, int) else ra[:, k, 0:t],
                                  rb[:, bass.ds(k, 1), 0:t].rearrange("p a t -> p (a t)") if not isinstance(k, int) else rb[:, k, 0:t],
                                  start, stop, False)
                    if stop and m < DC - 1:
                        last.then_inc(acc_mm, 1)
                last.then_inc(w_used, 1)

            def last_rows(n0, k, ra, rb, t):
                pe.wait_ge(lo_done, n0 + k + 2)
                for m in range(DC):
                    for kk in (k, k + 1):
                        s = (n0 + kk) % RING
                        ws = slice(m * P, (m + 1) * P)
                        last = triple(ps[bank_of(m)][:, 0:t], wH[:, s, ws], wL[:, s, ws], ra[:, kk, 0:t], rb[:, kk, 0:t],
                                      False, kk == k + 1, False)
                    if m < DC - 1:
                        last.then_inc(acc_mm, 1)
                last.then_inc(w_used, 2)

            def keep_busy(n):
                for _ in range(n):
                    mm(ps[7][:, 0:P], ident, cst[:, 0:P], start=True, stop=True, skip_group_check=True)

            def mean_squares(v):
                t = T_NORM[v]
                wait(pe, x_ready, x_count(v, 0))
                for i, m in enumerate(SUM_TILES):
                    if v > 0 and i == 2:
                        keep_busy(BUSY[0])
                    if i == 0:
                        pe.wait_ge(sq_four, 3 * (v + 1))
                    else:
                        pe.wait_ge(sq_pair, 2 * v + i)
                    for tb in range(t // P):
                        last = mm(ps[4][:, 2 * tb:2 * tb + 2], squares[m][:, tb * P:(tb + 1) * P], meanM[:, 0:2],
                                  start=(i == 0 and tb == 0), stop=(m == SUM_TILES[-1]), skip_group_check=True)
                last.then_inc(mean_mm, 1)
                if v > 0:
                    keep_busy(BUSY[1])

            def spread_roots(v):
                t = T_NORM[v]
                for hf in range(halves(t)):
                    cs = slice(hf * SEQ, (hf + 1) * SEQ)
                    pe.wait_ge(rms_diag, sum(T_NORM[:v]) // P + 2 * (hf + 1))
                    mm(ps[4][:, cs], meanM, T[:, 2, cs], start=True, stop=True, skip_group_check=True
                       ).then_inc(rms_row, 1)
                if v < 6:
                    keep_busy(BUSY[2])

            def norm_pe(v):
                mean_squares(v)
                spread_roots(v)

            def ffn(f, v):
                l, name = f // 2, "12"[f % 2]
                t = T_NORM[v]
                n0 = FIRST["wi" + name, l]

                def group(i, ada_base=None, turn_base=None):
                    static = isinstance(i, int)
                    first = static and n0 == i == 0
                    if static and i == 0:
                        wait(pe, x_ready, x_count(v, DC - 1))
                    else:
                        pe.wait_ge(a_out, i * 2 + 2 * GROUPS * f)
                    for j in range(4):
                        if j == 1 and not (static and i == 0):
                            pe.wait_ge(g_silu, i * 2 + 2 * GROUPS * f)
                        columns_piece(n0, j, 2 * (j % 2), j // 2, t, i, v if static and i == 0 and j in (0, 2) else None,
                                      (lambda: ada_turn(1)) if first and j == 1 else None)
                        if ada_base is not None:
                            if static:
                                ada_pair(j, ada_base + i)
                            else:
                                ada_pair(j, ada_base, i)
                        if turn_base is not None and j == 0:
                            if static:
                                ada_turn(turn_base + i - 1)
                            else:
                                ada_turn(turn_base - 1, i)
                        if first and j == 0:
                            for p in range(4):
                                ada_pair(p, 1)

                ada0, count, g0 = ADA_IN_FFN.get(f, (None, 0, 0))
                if g0:
                    group(0)
                if count:
                    pe.wait_ge(bank5_zero, f + 1)
                    group(g0, ada0 - g0)
                    with pe.Fori(g0 + 1, g0 + count) as i:
                        group(i, ada0 - g0, ada0 - g0)
                    group(g0 + count, None, ada0 - g0)
                else:
                    group(0)
                if g0 + count + 1 < GROUPS:
                    with pe.Fori(g0 + count + 1, GROUPS) as i:
                        group(i)
                n0 = FIRST["wo" + name, l]
                if count:
                    pe.wait_ge(ada_out, ada0 + count)

                def bank_wait(m):
                    if m == 4:
                        pe.wait_ge(a_out, 2 * GROUPS * (f + 1))
                    if m == 6:
                        pe.wait_ge(g_silu, 2 * GROUPS * (f + 1))
                pe.wait_ge(g_lo, 2 * GROUPS * (f + 1) - 2)
                for j in range(RING):
                    rows_piece(n0, j, j, GH, GL, t, j == 0, False, bank_wait=bank_wait if j == 0 else None)
                with pe.Fori(1, FC // RING) as i:
                    for j in range(RING):
                        rows_piece(n0, j, i * RING + j, GH, GL, t, False, False, i)
                pe.wait_ge(g_lo, 2 * GROUPS * (f + 1))
                last_rows(n0, FC - 2, GH, GL, t)

            def rope(l, bi):
                o = (bi + 1) % 5
                pe.wait_ge(proj_act, 26 * l + (1 if bi == 4 else 3 + bi))
                if o >= 2:
                    pe.wait_ge(rope_done, 5 * l + o - 1)
                mm(ps[4 + o % 2][:, 0:SEQ], rotM, T[:, min(bi, 3), 0:SEQ], start=True, stop=True).then_inc(rope_mm, 1)

            def unit_banks_free(l, u):
                if u >= 2:
                    p = u - 2
                    if p in ACT_UNITS:
                        pe.wait_ge(proj_act, 26 * l + 2 * ACT_UNITS.index(p) + 2)
                    else:
                        pe.wait_ge(proj_dve, 8 * l + 2 * DVE_UNITS.index(p) + 2)

            def scores(l, s):
                b, r = s // 2, s % 2
                rows = slice(r * HD, (r + 1) * HD)
                if s == 0:
                    pe.wait_ge(q_lo, 5 * (l + 1))
                    pe.wait_ge(v_lo, l + 1)
                for j in range(tiles(l)):
                    if s > 0:
                        pe.wait_ge(pt_lo, tile_count(l, s - 1, j))
                    for q in range(2 if j == 2 else 1):
                        tq = j + q
                        qs = slice(tq * P, (tq + 1) * P)
                        keys = slice(0, TOK) if j < 2 else slice(SEQ, TOK)
                        dst = ps[4 + j][:, 0:TOK] if j < 2 else ps[6][:, q * CTX:(q + 1) * CTX]
                        last = triple(dst, QH[rows, b, qs], QL[rows, b, qs], KH[rows, keys], KL[rows, keys], True, True)
                    last.then_inc(s_mm, 1)

            def transpose_probs(l, s):
                for j in range(tiles(l)):
                    pe.wait_ge(p_norm, tile_count(l, s, j))
                    for q in range(4):
                        src = T[:, j, q * P:(q + 1) * P] if j < 2 else \
                            T[:, 2, (q % 2) * CTX + (q // 2) * P:(q % 2) * CTX + (q // 2 + 1) * P]
                        last = nc.tensor.transpose(ps[4 + j][:, q * P:(q + 1) * P], src, ident)
                    last.then_inc(pt_mm, 1)

            def weigh_values(l, s):
                pe.wait_ge(pt_lo, tile_count(l, s, tiles(l) - 1))
                if s > 0:
                    pe.wait_ge(o_lo, 8 * l + s)
                for kb in range(4):
                    ks = slice(kb * P, (kb + 1) * P)
                    last = triple(ps[7][:, 0:SEQ].rearrange("p (t q) -> p t q", t=2), VH[:, kb, :], VL[:, kb, :],
                                  PTH[:, 0:2, ks], PTL[:, 0:2, ks], kb == 0, kb == 3)
                if l == 0:
                    for kb in range(2):
                        ks = slice(kb * CTX, (kb + 1) * CTX)
                        last = triple(ps[7][:, SEQ:TOK], VH[:, 2 + kb, :], VL[:, 2 + kb, :],
                                      PTH[:, 2, ks], PTL[:, 2, ks], kb == 0, kb == 1)
                last.then_inc(pv_mm, 1)

            def mixers(l):
                v = 3 * l + 1
                t = TOK if l == 0 else SEQ
                n0 = FIRST["proj", l]
                pe.wait_ge(x_ready, x_count(v, DC - 1))
                for h in range(PROJ_P):
                    u, kh = h // 2, h % 2
                    if h == 3:
                        rope(l, 4)
                        pe.wait_ge(proj_act, 26 * l + 2)
                        for tb in range(4):
                            last = nc.tensor.transpose(ps[6][:, tb * P:(tb + 1) * P], V32[:, tb * P:(tb + 1) * P],
                                                       ident)
                        last.then_inc(v_T, 1)
                    if h in (5, 7):
                        rope(l, h - 5)
                        rope(l, h - 4)
                    s, stage = divmod(h - HEAD0, 3)
                    if stage == 0 and 1 <= s <= HEADS:
                        weigh_values(l, s - 1)
                    if stage == 0 and 0 <= s < HEADS:
                        scores(l, s)
                    if stage == 2 and 0 <= s < HEADS:
                        transpose_probs(l, s)
                    if kh == 0:
                        unit_banks_free(l, u)
                    columns_piece(n0 + h, 0, 2 * (u % 2), kh, TOK if UNITS[u] == "kv" else t, v=v if u == 0 else None)

                def oa_bank(m):
                    if m == 0:
                        pe.wait_ge(o_lo, 8 * (l + 1))
                        pe.wait_ge(proj_act, 26 * (l + 1))
                for k in range(4):
                    rows_piece(FIRST["oa", l] + k, 0, k, QH, QL, t, k == 0, k == 3, bank_wait=oa_bank if k == 0 else None)

                def ob_bank(m):
                    pe.wait_ge(oa_out, 8 * l + m + 1)
                pe.wait_ge(y_lo, 4 * (l + 1))
                for k in range(4):
                    rows_piece(FIRST["ob", l] + k, 0, k, YH, YL, t, k == 0, k == 3, bank_wait=ob_bank if k == 0 else None)

                def out_bank(m):
                    pe.wait_ge(ob_out, 8 * l + m + 1)
                for k in range(DC - 2):
                    pe.wait_ge(m_lo, 8 * l + k + 1)
                    rows_piece(FIRST["out", l] + k, 0, k, hH, hL, t, k == 0, False,
                               bank_wait=out_bank if k == 0 else None)
                pe.wait_ge(m_lo, 8 * (l + 1))
                last_rows(FIRST["out", l], DC - 2, hH, hL, t)

            pe.wait_ge(in_c, 16)
            pe.wait_ge(in_vec, 16 * 7)
            nc.tensor.transpose(ps[6][:, 0:96], vin[0:96, 0, :], ident[0:96, 0:96])
            for l in range(DEPTH):
                last = nc.tensor.transpose(ps[6][:, 96 + 72 * l:96 + 72 * (l + 1)], vin[0:72, 1 + l, :],
                                           ident[0:72, 0:72])
            last.then_inc(vec_T, 1)
            pe.wait_ge(in_x, 32)
            for m in range(DC):
                if m >= 4:
                    pe.wait_ge(x_ready, m - 3)
                for tb in range(4):
                    last = nc.tensor.transpose(ps[m % 4][:, tb * P:(tb + 1) * P], xin[:, tb, m * P:(m + 1) * P], ident)
                last.then_inc(x_T, 1)
            mean_squares(0)
            pe.wait_ge(c_silu, 1)
            pe.wait_ge(bank5_zero, 1)
            pe.wait_ge(vec_out, 1)
            for p in range(4):
                ada_pair(p, 0)
            spread_roots(0)
            ada_turn(0)

            for l in range(DEPTH):
                ffn(2 * l, 3 * l)
                norm_pe(3 * l + 1)
                mixers(l)
                norm_pe(3 * l + 2)
                ffn(2 * l + 1, 3 * l + 2)
                norm_pe(3 * l + 3)
            for m in range(DC):
                pe.wait_ge(fin_ready, m + 1)
                for tb in range(2):
                    nc.tensor.transpose(ps[2 * tb + m // 4][:, (m % 4) * P:(m % 4 + 1) * P],
                                        T[:, m % 2, tb * P:(tb + 1) * P], ident).then_inc(fin_T, 1)

        @block.scalar
        def _(act):
            av = nc.scalar.activation

            def hi(n0, j=0, i=0):
                s = (n0 + j) % RING
                if n0 + j >= PIECES and isinstance(i, int):
                    return
                if isinstance(i, int):
                    act.wait_ge(loaded[s], LOADED[n0 + j + 4 * i])
                    wait(act, w_used, n0 + j + 4 * i - RING + 1)
                else:
                    act.wait_ge(loaded[s], i * 16 + LOADED[n0 + j])
                    act.wait_ge(w_used, i * 4 + (n0 + j - RING + 1))
                av(wH[:, s, :], raw[:, s, :], ACT.Copy).then_inc(hi_done, 1)

            def roots_act(v):
                t = T_NORM[v]
                for m in range(DC):
                    act.wait_ge(x_ready, x_count(v, m))
                    av(squares[m][:, 0:t], X[:, m, 0:t], ACT.Square).then_inc(sq_done, 1)
                act.wait_ge(mean_mm, v + 1)
                nb = 2 * t // P
                av(root[:, 0, 0:nb], ps[4][:, 0:nb], ACT.Sqrt, bias=epsT[:, 0:1]).then_inc(rms, 1)

            def shift_act(v, n0):
                t = T_NORM[v]
                shift = 9 * (v // 3) + 3 * (v % 3)
                for m in range(DC):
                    for hf in range(halves(t)):
                        c0 = h_count(v, m) - halves(t) + hf + 1
                        cs = slice(hf * SEQ, (hf + 1) * SEQ)
                        act.wait_ge(hp_done, c0)
                        av(hH[:, m, cs], T[:, m % 2, cs], ACT.Identity, bias=mod[:, shift, m, hf:hf + 1]).then_inc(h_hi, 1)
                    if m == 3:
                        hi(n0 + 2)
                    if m == 6:
                        hi(n0 + 3)

            def silu_evac(f, t, i):
                static = isinstance(i, int)
                for b in range(2):
                    act.wait_ge(w_used, i * RING + (FIRST["wi" + "12"[f % 2], f // 2] + 4))
                    wait(act, g_lo, i * 2 + 2 * GROUPS * f)
                    av(T[:, 2 + b, 0:t], ps[2 + b][:, 0:t], ACT.Silu).then_inc(g_silu, 1)
                for b in range(2):
                    act.wait_ge(g_prod, i * 2 + (2 * GROUPS * f + b + 1))
                    if static:
                        dst = GH[:, 2 * i + b, 0:t]
                    else:
                        dst = GH[:, bass.ds(i * 2 + b, 1), 0:t].rearrange("p a t -> p (a t)")
                    av(dst, T[:, 2 + b, 0:t], ACT.Copy).then_inc(g_hi, 1)

            def ffn_act(f, v):
                l, name = f // 2, "12"[f % 2]
                t = T_NORM[v]
                n0 = FIRST["wi" + name, l]

                n0w = n0

                def value_evac(i):
                    for b in range(2):
                        act.wait_ge(w_used, i * RING + (n0w + 3))
                        av(T[:, b, 0:t], ps[b][:, 0:t], ACT.Copy).then_inc(a_out, 1)

                def group(i):
                    hi(n0, 2, i)
                    hi(n0, 3, i)
                    silu_evac(f, t, i - 1)
                    hi(n0, 4, i)
                    hi(n0, 5, i)
                    value_evac(i)
                hi(n0, 4)
                hi(n0, 5)
                value_evac(0)
                group(1)
                with act.Fori(2, GROUPS - 1) as i:
                    group(i)
                i = GROUPS - 1
                hi(n0 + 4 * i + 2)
                hi(n0 + 4 * i + 3)
                silu_evac(f, t, i - 1)
                hi(n0 + 4 * i + 4)
                hi(n0 + 4 * i + 5)
                value_evac(i)
                silu_evac(f, t, i)
                n0 = FIRST["wo" + name, l]
                with act.Fori(0, FC // RING) as i:
                    for j in range(RING):
                        hi(n0, 2 + j, i)
                for j in range(FC // RING * RING, FC):
                    hi(n0 + 2 + j)

            def mixers_act(l):
                t = TOK if l == 0 else SEQ
                n0 = FIRST["proj", l]
                a0 = 26 * l
                def probs(s):
                    h = HEADS * l + STEP_HEAD[s]
                    for j in range(tiles(l)):
                        act.wait_ge(s_max, tile_count(l, s, j))
                        for q in range(2 if j == 2 else 1):
                            cs = slice(0, TOK) if j < 2 else slice(q * CTX, (q + 1) * CTX)
                            av(T[:, j, cs], ps[4 + j][:, cs], ACT.Exp, bias=stat[:, 1, j + q:j + q + 1], scale=SCALE,
                               accum_out=stat[:, 2, j + q:j + q + 1]).then_inc(p_exp, 1)
                    nq = 4 if l == 0 else 2
                    av(stat[:, 3, 0:nq], stat[:, 1, 0:nq], ACT.Exp, bias=sinkP[:, h:h + 1]).then_inc(p_exp, 1)

                def turned_probs(s):
                    for j in range(tiles(l)):
                        act.wait_ge(pt_mm, tile_count(l, s, j))
                        av(PTH[:, j, :], ps[4 + j][:], ACT.Copy).then_inc(pt_hi, 1)

                def head_out(s):
                    act.wait_ge(pv_mm, 8 * l + s + 1)
                    rows = slice((s % 2) * HD, (s % 2 + 1) * HD)
                    av(QH[rows, s // 2, 0:t], ps[7][rows, 0:t], ACT.Copy).then_inc(o_hi, 1)

                def unit_evac(u):
                    kind = UNITS[u]
                    act.wait_ge(w_used, n0 + 2 * u + 2)
                    banks = [ps[2 * (u % 2) + b] for b in range(2)]
                    if kind == "kv":
                        av(T[:, 3, :], banks[0][:], ACT.Copy).then_inc(proj_act, 1)
                        av(V32[:], banks[1][:], ACT.Copy).then_inc(proj_act, 1)
                    elif kind[0] == "q":
                        for b in range(2):
                            bi = 2 * int(kind[1]) + b
                            if bi == 3:
                                act.wait_ge(q_lo, 5 * l + 1)
                            av(T[:, bi, 0:t], banks[b][:, 0:t], ACT.Copy).then_inc(proj_act, 1)
                    elif kind[0] == "c":
                        if kind == "c1":
                            act.wait_ge(y_lo, 4 * l + 2)
                        for b in range(2):
                            av(cC[:, b, 0:t], banks[b][:, 0:t], ACT.Copy).then_inc(proj_act, 1)
                    else:
                        i = int(kind[1])
                        if i == 4:
                            act.wait_ge(y_lo, 4 * l + 4)
                        G = GA if i < 4 else GB
                        for b in range(2):
                            av(G[:, 2 * (i % 4) + b, 0:t], banks[b][:, 0:t], ACT.Tanh, scale=0.5
                               ).then_inc(proj_act, 1)

                def conv_high(pair):
                    for b in range(2):
                        act.wait_ge(proj_dve, 8 * l + 2 * DVE_UNITS.index(5 + 3 * pair) + b + 1)
                        av(YH[:, 2 * pair + b, 0:t], cY[:, b, 0:t], ACT.Copy).then_inc(y_hi, 1)

                for h in range(PROJ_P + 1):
                    if 2 <= h < PROJ_P:
                        hi(n0 + h + 2)
                    s, stage = divmod(h - HEAD0, 3)
                    if stage == 0 and 1 <= s <= HEADS:
                        head_out(s - 1)
                    if stage == 0 and 0 <= s < HEADS:
                        probs(s)
                    if stage == 2 and 0 <= s < HEADS:
                        turned_probs(s)
                    if h == 3:
                        act.wait_ge(rope_done, 5 * l + 1)
                        av(KH[:], T[:, 3, :], ACT.Copy).then_inc(q_hi, 1)
                        act.wait_ge(v_T, l + 1)
                        av(VH[:].rearrange("p b d -> p (b d)"), ps[6][:], ACT.Copy).then_inc(v_hi, 1)
                    if h in (5, 7):
                        for bi in (h - 5, h - 4):
                            act.wait_ge(rope_done, 5 * l + bi + 2)
                            av(QH[:, bi, 0:t], T[:, bi, 0:t], ACT.Copy).then_inc(q_hi, 1)
                    if h in (13, 19):
                        conv_high((h - 13) // 6)
                    if h % 2 == 0 and h >= 2 and h // 2 - 1 in ACT_UNITS:
                        unit_evac(h // 2 - 1)
                for n in range(FIRST["oa", l] + 2, FIRST["out", l] + 2):
                    hi(n)
                for m in range(DC):
                    act.wait_ge(ob_sum, 8 * l + m + 1)
                    av(hH[:, m, 0:t], GB[:, m, 0:t], ACT.Copy).then_inc(m_hi, 1)
                    if m in (0, 3):
                        hi(FIRST["out", l] + 2 + m // 3)
                for n in range(FIRST["out", l] + 4, FIRST["out", l] + DC + 2):
                    hi(n)

            act.wait_ge(vec_out, 1)
            act.wait_ge(vec_step, 1)
            av(cact[:].rearrange("p v k -> p (v k)"), VT[:, V_C:V_C + 16], ACT.Silu).then_inc(c_silu, 1)
            roots_act(0)
            hi(0)
            hi(1)
            for l in range(DEPTH):
                shift_act(3 * l, FIRST["wi1", l])
                ffn_act(2 * l, 3 * l)
                roots_act(3 * l + 1)
                shift_act(3 * l + 1, FIRST["proj", l])
                mixers_act(l)
                roots_act(3 * l + 2)
                shift_act(3 * l + 2, FIRST["wi2", l])
                ffn_act(2 * l + 1, 3 * l + 2)
                roots_act(3 * l + 3)

        @block.vector
        def _(dve):
            tt, ts, stt = nc.vector.tensor_tensor, nc.vector.tensor_scalar, nc.vector.scalar_tensor_tensor
            steps = [0]

            def mark(ins):
                steps[0] += 1
                ins.then_inc(vec_step, 1)

            def settle():
                dve.wait_ge(vec_step, steps[0])

            def lo(n0, j=0, i=0):
                s = (n0 + j) % RING
                if n0 + j >= PIECES and isinstance(i, int):
                    return
                dve.wait_ge(hi_done, i * 4 + (n0 + j + 1))
                tt(wL[:, s, :], raw[:, s, :], wH[:, s, :].bitcast(F32), ALU.subtract).then_inc(lo_done, 1)

            def rows_evac(base, i=None):
                dve.wait_ge(ada_used, 4 * (base + 1) if i is None else i * 4 + 4 * (base + 1))
                if i is not None or base > 0:
                    dve.wait_ge(ada_T, base if i is None else i + base)
                nc.vector.tensor_copy(rowS[:], ps[5][:]).then_inc(row_out, 1)

            def ada_evac(base, i=None):
                dve.wait_ge(ada_T, base + 1 if i is None else i + (base + 1))
                if i is None:
                    dst = mod[:, 0:2, 4 * base:4 * base + 4]
                    bias = VT[:, V_BADA:V_BADA + 2 * DC].rearrange("p (j k) -> p j k", j=2)[:, :, 4 * base:4 * base + 4]
                else:
                    dst = mod[:, bass.ds(i + base, 1)].rearrange("p a (h q) v -> p (a h) q v", h=2)
                    bias = VT[:, bass.ds(i * DC + (V_BADA + base * DC), DC)].rearrange("p (h q) -> p h q", h=2)
                part = ps[6][:].rearrange("p (q e h r) -> p h q e r", q=4, e=2, h=2)
                bias = bias.unsqueeze(3).broadcast_to([P, 2, 4, 2])
                tt(dst, part[:, :, :, 0, 0:2], bias, ALU.add).then_inc(ada_part, 1)
                dve.wait_ge(ada_part, base + 1 if i is None else i + (base + 1))
                tt(dst, part[:, :, :, 1, 0:2], dst, ALU.add).then_inc(ada_out, 1)

            def roots_dve(v):
                t = T_NORM[v]
                if v == 0:
                    add_pair(v, 4)
                add_pair(v, 6)
                dve.wait_ge(rms, v + 1)
                nb = 2 * t // P
                mark(nc.vector.reciprocal(root[:, 1, 0:nb], root[:, 0, 0:nb]))
                settle()
                for tb in range(t // P):
                    ts(T[:, 2, tb * P:(tb + 1) * P], ident, root[:, 1, 2 * tb:2 * tb + 1], float(D),
                       ALU.mult, ALU.mult).then_inc(rms_diag, 1)

            def scale_vector(v, need=None, ks=slice(0, DC)):
                mi = 9 * (v // 3) + 3 * (v % 3)
                dve.wait_ge(ada_out, mi + 2 if need is None else need)
                nk = ks.stop - ks.start
                mark(stt(normA[:, v, ks], mod[:, mi + 1, ks], 1.0,
                         VT[:, V_NORM + v * DC + ks.start:V_NORM + v * DC + ks.stop].unsqueeze(2
                                                                                 ).broadcast_to([P, nk, 2]),
                         ALU.add, ALU.mult))
                settle()

            def final_scale():
                t = T_NORM[6]
                dve.wait_ge(rms_row, sum(T_NORM) // SEQ)
                for m in range(DC):
                    if m >= 2:
                        dve.wait_ge(fin_T, 2 * (m - 1))
                    stt(T[:, m % 2, 0:t], X[:, m, 0:t], VT[:, V_FIN + m:V_FIN + m + 1], ps[4][:, 0:t],
                        ALU.mult, ALU.mult).then_inc(fin_ready, 1)

            def scale_dve(v, n0):
                t = T_NORM[v]
                mi = 9 * (v // 3) + 3 * (v % 3)
                dve.wait_ge(rms_row, sum(T_NORM[:v + 1]) // SEQ)

                def scaled(m):
                    for hf in range(halves(t)):
                        cs = slice(hf * SEQ, (hf + 1) * SEQ)
                        stt(T[:, m % 2, cs], X[:, m, cs], normA[:, v, m, hf:hf + 1], ps[4][:, cs],
                            ALU.mult, ALU.mult).then_inc(hp_done, 1)

                def low(m):
                    for hf in range(halves(t)):
                        cs = slice(hf * SEQ, (hf + 1) * SEQ)
                        dve.wait_ge(h_hi, h_count(v, m) - halves(t) + hf + 1)
                        stt(hL[:, m, cs], T[:, m % 2, cs], mod[:, mi, m, hf:hf + 1], hH[:, m, cs].bitcast(F32),
                            ALU.add, ALU.subtract).then_inc(h_lo, 1)
                scaled(0)
                for m in range(DC):
                    if v == 0 and m == 1:
                        lo(1)
                    if v == 0 and m == 3:
                        low(m)
                        rows_evac(1)
                        ada_evac(1)
                        scale_vector(0, 2, slice(4, DC))
                    if m + 1 < DC:
                        if m >= 1:
                            dve.wait_ge(h_lo, h_count(v, m - 1))
                        scaled(m + 1)
                    if v > 0 or m != 3:
                        low(m)
                    if m == 3:
                        lo(n0 + 2)
                    if m == 6:
                        lo(n0 + 3)

            def add_pair(v, m):
                t = T_NORM[v]
                dve.wait_ge(sq_done, DC * v + m + 2)
                tt(squares[m][:, 0:t], squares[m][:, 0:t], squares[m + 1][:, 0:t], ALU.add).then_inc(sq_pair, 1)

            def residual(r):
                t = T_AFTER[r]
                l, q = (r - 1) // 3, (r - 1) % 3
                mi = 9 * l + 3 * q + 2
                dve.wait_ge(ada_out, mi + 1)
                mark(ts(gateH[:, r - 1], mod[:, mi], 0.5, None, ALU.mult))
                settle()
                for m in range(DC):
                    wait_chunk(dve, l, ("wo1", "out", "wo2")[q], m)
                    for hf in range(halves(t)):
                        cs = slice(hf * SEQ, (hf + 1) * SEQ)
                        stt(X[:, m, cs], ps[bank_of(m)][:, cs], gateH[:, r - 1, m, hf:hf + 1], X[:, m, cs],
                            ALU.mult, ALU.add).then_inc(x_ready, 1)
                    if m == 6:
                        add_pair(r, 4)

            def product(f, t, i):
                for b in range(2):
                    dve.wait_ge(g_silu, i * 2 + (2 * GROUPS * f + b + 1))
                    dve.wait_ge(a_out, i * 2 + (2 * GROUPS * f + b + 1))
                    tt(T[:, 2 + b, 0:t], T[:, 2 + b, 0:t], T[:, b, 0:t], ALU.mult).then_inc(g_prod, 1)
                for b in range(2):
                    dve.wait_ge(g_hi, i * 2 + (2 * GROUPS * f + b + 1))
                    if isinstance(i, int):
                        high, low = GH[:, 2 * i + b, 0:t], GL[:, 2 * i + b, 0:t]
                    else:
                        high = GH[:, bass.ds(i * 2 + b, 1), 0:t].rearrange("p a t -> p (a t)")
                        low = GL[:, bass.ds(i * 2 + b, 1), 0:t].rearrange("p a t -> p (a t)")
                    tt(low, T[:, 2 + b, 0:t], high.bitcast(F32), ALU.subtract).then_inc(g_lo, 1)

            def ffn_dve(f, v):
                l, name = f // 2, "12"[f % 2]
                t = T_NORM[v]
                n0 = FIRST["wi" + name, l]

                def group(i, ada0=None):
                    if ada0 is not None:
                        rows_evac(ada0 - 1, i)
                    lo(n0, 2, i)
                    lo(n0, 3, i)
                    product(f, t, i - 1)
                    if ada0 is not None:
                        ada_evac(ada0 - 1, i)
                    lo(n0, 4, i)
                    lo(n0, 5, i)
                lo(n0, 4)
                lo(n0, 5)
                ada0, count, g0 = ADA_IN_FFN.get(f, (None, 0, 0))
                if g0:
                    group(1)
                if count:
                    with dve.Fori(g0 + 1, g0 + count + 1) as i:
                        group(i, ada0 - g0)
                if g0 + count + 1 < GROUPS - 1:
                    with dve.Fori(g0 + count + 1, GROUPS - 1) as i:
                        group(i)
                i = GROUPS - 1
                lo(n0 + 4 * i + 2)
                lo(n0 + 4 * i + 3)
                product(f, t, i - 1)
                lo(n0 + 4 * i + 4)
                lo(n0 + 4 * i + 5)
                product(f, t, i)
                n0 = FIRST["wo" + name, l]
                with dve.Fori(0, FC // RING) as i:
                    for j in range(RING):
                        lo(n0, 2 + j, i)
                for j in range(FC // RING * RING, FC):
                    lo(n0 + 2 + j)

            def rope_dve(l, bis):
                t = TOK if l == 0 else SEQ
                for bi in bis:
                    o = (bi + 1) % 5
                    dve.wait_ge(rope_mm, 5 * l + o + 1)
                    w = T[:, min(bi, 3), 0:SEQ]
                    mark(tt(ropeT[:, bi % 2, :], ps[4 + o % 2][:, 0:SEQ], sinT, ALU.mult))
                    mark(tt(w, w, cosT, ALU.mult))
                    settle()
                    tt(w, w, ropeT[:, bi % 2, :], ALU.add).then_inc(rope_done, 1)
                for bi in bis:
                    dve.wait_ge(q_hi, 5 * l + (bi + 1) % 5 + 1)
                    if bi < 4:
                        tt(QL[:, bi, 0:t], T[:, bi, 0:t], QH[:, bi, 0:t].bitcast(F32), ALU.subtract).then_inc(q_lo, 1)
                    else:
                        tt(KL[:], T[:, 3, :], KH[:].bitcast(F32), ALU.subtract).then_inc(q_lo, 1)

            def conv_taps(l, pair):
                segs = 2 if l == 0 else 1
                for k in range(CONV_K):
                    for b in range(2):
                        tap = VT[:, V_CONV + (l * CONV_K + k) * CC + 2 * pair + b:][:, 0:1]
                        src = cU[:, b, 0:segs, k:k + SEQ]
                        dst = cY[:, b, 0:segs * SEQ].rearrange("p (s t) -> p s t", s=segs)
                        if k == 0:
                            mark(ts(dst, src, tap, None, ALU.mult))
                        else:
                            mark(stt(dst, src, tap, dst, ALU.mult, ALU.add))
                    settle()

            def y_low(l, pair, t):
                for b in range(2):
                    dve.wait_ge(y_hi, 4 * l + 2 * pair + b + 1)
                    tt(YL[:, 2 * pair + b, 0:t], cY[:, b, 0:t], YH[:, 2 * pair + b, 0:t].bitcast(F32),
                       ALU.subtract).then_inc(y_lo, 1)

            def mixers_dve(l):
                t = TOK if l == 0 else SEQ
                segs = t // SEQ
                n0 = FIRST["proj", l]
                mark(nc.vector.memset(cU[:].rearrange("p a b c -> p (a b c)"), 0.0))
                settle()
                def unit_evac(u):
                    kind = UNITS[u]
                    dve.wait_ge(w_used, n0 + 2 * u + 2)
                    banks = [ps[2 * (u % 2) + b] for b in range(2)]
                    if kind[0] == "u":
                        dve.wait_ge(proj_act, 26 * l + 2 * ACT_UNITS.index(u - 1) + 2)
                        for b in range(2):
                            tt(cU[:, b, 0:segs, 1:SEQ + 1], banks[b][:, 0:t].rearrange("p (s t) -> p s t", s=segs),
                               cC[:, b, 0:t].rearrange("p (s t) -> p s t", s=segs), ALU.mult).then_inc(proj_dve, 1)
                        dve.wait_ge(proj_dve, 8 * l + 2 * DVE_UNITS.index(u) + 2)
                        conv_taps(l, int(kind[1]))
                    else:
                        for b in range(2):
                            w = cY[:, b, 0:t]
                            tt(w, banks[b][:, 0:t], w, ALU.mult).then_inc(proj_dve, 1)

                def maxima(s):
                    h = HEADS * l + STEP_HEAD[s]
                    for j, (edge, cs) in enumerate(((mask0, slice(P, 2 * P)), (mask1, slice(0, P)))):
                        dve.wait_ge(s_mm, tile_count(l, s, j))
                        mark(tt(ps[4 + j][:, cs], ps[4 + j][:, cs], edge, ALU.add))
                    for j in range(tiles(l)):
                        if j == 2:
                            dve.wait_ge(s_mm, tile_count(l, s, 2))
                            nq, src = 2, ps[6][:].rearrange("p (q k) -> p q k", q=2)
                        else:
                            if j == 0:
                                settle()
                            nq, src = 1, ps[4 + j][:]
                        mark(nc.vector.tensor_reduce(stat[:, 0, j:j + nq], src, AX_X, ALU.max))
                        settle()
                        ts(stat[:, 1, j:j + nq], stat[:, 0, j:j + nq], -SCALE, sinkN[:, h:h + 1], ALU.mult, ALU.min
                           ).then_inc(s_max, 1)

                def normalise(s):
                    nq = 4 if l == 0 else 2
                    dve.wait_ge(p_exp, (nq + 1) * (s + 1) + (40 if l else 0))
                    mark(tt(stat[:, 4, 0:nq], stat[:, 2, 0:nq], stat[:, 3, 0:nq], ALU.add))
                    settle()
                    mark(nc.vector.reciprocal(stat[:, 5, 0:nq], stat[:, 4, 0:nq]))
                    settle()
                    for j in range(tiles(l)):
                        for q in range(2 if j == 2 else 1):
                            cs = slice(0, TOK) if j < 2 else slice(q * CTX, (q + 1) * CTX)
                            ins = ts(T[:, j, cs], T[:, j, cs], stat[:, 5, j + q:j + q + 1], None, ALU.mult)
                            if j == 2 and q == 0:
                                mark(ins)
                                settle()
                            else:
                                ins.then_inc(p_norm, 1)

                def turned_probs(s):
                    for j in range(tiles(l)):
                        dve.wait_ge(pt_hi, tile_count(l, s, j))
                        tt(PTL[:, j, :], ps[4 + j][:], PTH[:, j, :].bitcast(F32), ALU.subtract).then_inc(pt_lo, 1)

                def head_out(s):
                    dve.wait_ge(o_hi, 8 * l + s + 1)
                    rows = slice((s % 2) * HD, (s % 2 + 1) * HD)
                    tt(QL[rows, s // 2, 0:t], ps[7][rows, 0:t], QH[rows, s // 2, 0:t].bitcast(F32),
                       ALU.subtract).then_inc(o_lo, 1)

                for h in range(PROJ_P):
                    s, stage = divmod(h - HEAD0, 3)
                    if stage == 1 and 0 <= s < HEADS:
                        normalise(s)
                    if h >= 2:
                        lo(n0 + h + 2)
                    if stage == 0 and 1 <= s <= HEADS:
                        head_out(s - 1)
                    if stage == 0 and 0 <= s < HEADS:
                        maxima(s)
                    if stage == 2 and 0 <= s < HEADS:
                        turned_probs(s)
                    if h == 3:
                        rope_dve(l, (4,))
                        dve.wait_ge(v_hi, l + 1)
                        tt(VL[:].rearrange("p b d -> p (b d)"), ps[6][:],
                           VH[:].rearrange("p b d -> p (b d)").bitcast(F32), ALU.subtract).then_inc(v_lo, 1)
                    if h in (5, 7):
                        rope_dve(l, (h - 5, h - 4))
                    if h in (13, 19):
                        y_low(l, (h - 13) // 6, t)
                    if h % 2 == 0 and h >= 2 and h // 2 - 1 in DVE_UNITS:
                        unit_evac(h // 2 - 1)
                for n in range(FIRST["oa", l] + 2, FIRST["oa", l] + 6):
                    lo(n)
                for m in range(DC):
                    wait_chunk(dve, l, "oa", m)
                    stt(GA[:, m, 0:t], GA[:, m, 0:t], 1.0, ps[bank_of(m)][:, 0:t], ALU.add, ALU.mult
                        ).then_inc(oa_out, 1)
                for n in range(FIRST["ob", l] + 2, FIRST["ob", l] + 6):
                    lo(n)
                dve.wait_ge(oa_out, 8 * (l + 1))

                def branch_gate(m):
                    wait_chunk(dve, l, "ob", m)
                    stt(GB[:, m, 0:t], GB[:, m, 0:t], 1.0, ps[bank_of(m)][:, 0:t], ALU.add, ALU.mult
                        ).then_inc(ob_out, 1)

                def branch_sum(m):
                    dve.wait_ge(ob_out, 8 * l + m + 1)
                    tt(GB[:, m, 0:t], GB[:, m, 0:t], GA[:, m, 0:t], ALU.add).then_inc(ob_sum, 1)

                def branch_low(m):
                    dve.wait_ge(m_hi, 8 * l + m + 1)
                    tt(hL[:, m, 0:t], GB[:, m, 0:t], hH[:, m, 0:t].bitcast(F32), ALU.subtract).then_inc(m_lo, 1)
                branch_gate(0)
                branch_gate(1)
                branch_sum(0)
                branch_gate(2)
                branch_low(0)
                for m in range(3, DC):
                    branch_gate(m)
                lo(FIRST["out", l] + 2)
                branch_sum(1)
                for m in range(1, DC):
                    if m + 1 < DC:
                        branch_sum(m + 1)
                    branch_low(m)
                    if m == 3:
                        lo(FIRST["out", l] + 3)
                for n in range(FIRST["out", l] + 4, FIRST["out", l] + DC + 2):
                    lo(n)

            nc.vector.memset(ps[5][:], 0.0).then_inc(bank5_zero, 1)
            dve.wait_ge(vec_T, 1)
            nc.vector.tensor_copy(VT[:], ps[6][:, 0:NVEC]).then_inc(vec_out, 1)
            mark(nc.vector.memset(epsT[:], EPS))
            for m in range(DC):
                dve.wait_ge(x_T, m + 1)
                nc.vector.tensor_copy(X[:, m, :], ps[m % 4][:]).then_inc(x_ready, 1)
            roots_dve(0)
            dve.wait_ge(in_sink, 16)
            mark(ts(sinkN[:], sinkP[:], -1.0, None, ALU.mult))
            dve.wait_ge(vec_out, 1)
            lo(0)
            rows_evac(0)
            ada_evac(0)
            scale_vector(0, 1, slice(0, 4))
            for l in range(DEPTH):
                if l > 0:
                    scale_vector(3 * l)
                scale_dve(3 * l, FIRST["wi1", l])
                ffn_dve(2 * l, 3 * l)
                residual(3 * l + 1)
                scale_vector(3 * l + 1)
                roots_dve(3 * l + 1)
                scale_dve(3 * l + 1, FIRST["proj", l])
                mixers_dve(l)
                residual(3 * l + 2)
                if l == 0:
                    dve.wait_ge(x_ready, x_count(2, DC - 1))
                    nc.vector.memset(ps[5][:], 0.0).then_inc(bank5_zero, 1)
                scale_vector(3 * l + 2)
                roots_dve(3 * l + 2)
                scale_dve(3 * l + 2, FIRST["wi2", l])
                ffn_dve(2 * l + 1, 3 * l + 2)
                residual(3 * l + 3)
                roots_dve(3 * l + 3)
            final_scale()
            for tb in range(2):
                for half in range(2):
                    dve.wait_ge(fin_T, 2 * DC if half else DC - 1 + tb)
                    nc.vector.tensor_copy(yout[:, tb, half * TOK:(half + 1) * TOK], ps[2 * tb + half][:]
                                          ).then_inc(fin_out, 1)


_INS = ["x", "c", "ctx", "c_ctx", "w_ada", "b_ada", "norm_w", "ffn1_wi", "ffn1_wo", "w_in", "conv_w", "sink", "w_oa",
        "w_ob", "w_out", "ffn2_wi", "ffn2_wo", "final_norm_w"]


def kernel(**inputs):
    import concourse.bacc as bacc
    from concourse.bass_utils import run_bass_kernel_spmd

    nc = bacc.Bacc("TRN2", target_bir_lowering=False, num_devices=1)
    arrays, args = {}, []
    for name in _INS + ["shape_consts"]:
        a = shape_constants() if name == "shape_consts" else np.ascontiguousarray(inputs[name])
        arrays[f"in_{name}"] = a
        args.append(nc.dram_tensor(f"in_{name}", a.shape, mybir.dt.from_np(a.dtype), kind="ExternalInput").ap())
    args.append(nc.dram_tensor("out", (1, SEQ, D), F32, kind="ExternalOutput").ap())
    build(nc, *args)
    r = run_bass_kernel_spmd(nc, [arrays], core_ids=[0])
    return r.results[0]["out"]
```
